# Optimizing a Trainium2 kernel written in Bass

```python
import math
import jax, jax.numpy as jnp
from jax import lax
import numpy as np

D_MODEL = 1024
BATCH = 1
SEQ = 256
DEPTH = 1

GRID_W = 64
CTX_LEN = 256
HEAD_DIM = 64
A_HEADS = 4
R_HEADS = 4
R_DK = 64
R_DV = 128
A_QK = A_HEADS * 2 * HEAD_DIM
A_V = A_HEADS * 2 * HEAD_DIM
R_QK = R_HEADS * R_DK
R_V = R_HEADS * R_DV
D_IN = 2 * A_QK + A_V + 2 * R_QK + 2 * R_V
D_MIX = A_V + R_V
Q_BLOCK = 128
RET_CHUNK = 128
ROPE_BASE = 10000.0
N_EXPERTS = 64
N_GROUPS = 8
TOPK_GROUPS = 4
TOP_K = 8
D_EXPERT = D_MODEL // 4
D_SHARED = D_MODEL // 4
ROUTED_SCALE = 2.5
MOE_BLOCK = 128
NORM_EPS = 1e-6


def rmsnorm(x, g):
    xf = x.astype(jnp.float32)
    y = xf * lax.rsqrt(jnp.mean(xf * xf, axis=-1, keepdims=True) + NORM_EPS)
    return (y * g.astype(jnp.float32)).astype(x.dtype)

def modulate(h, shift, scale):
    return h * (1 + scale[:, None]) + shift[:, None]

def axial_rope_tables(n_tokens):
    n_rows = n_tokens // GRID_W
    rows = jnp.broadcast_to(jnp.arange(n_rows, dtype=jnp.float32)[:, None], (n_rows, GRID_W)).reshape(-1)
    cols = jnp.broadcast_to(jnp.arange(GRID_W, dtype=jnp.float32)[None, :], (n_rows, GRID_W)).reshape(-1)
    n_freq = HEAD_DIM // 4
    inv_freq = ROPE_BASE ** (-jnp.arange(n_freq, dtype=jnp.float32) / n_freq)
    ang = jnp.stack([rows[:, None] * inv_freq, cols[:, None] * inv_freq], axis=1)
    return jnp.cos(ang), jnp.sin(ang)

def apply_axial_rope(x, cos, sin):
    n_freq = HEAD_DIM // 4
    xr = x.reshape(x.shape[:-1] + (2, 2, n_freq)).astype(jnp.float32)
    shp = (cos.shape[0],) + (1,) * (x.ndim - 3) + (2, n_freq)
    c = cos.reshape(shp)
    s = sin.reshape(shp)
    x1, x2 = xr[..., 0, :], xr[..., 1, :]
    out = jnp.stack([x1 * c - x2 * s, x1 * s + x2 * c], axis=-2)
    return out.reshape(x.shape).astype(x.dtype)

def project_heads(h, w_in):
    bn, t, _ = h.shape
    p = h @ w_in
    sizes = (A_QK, A_QK, A_V, R_QK, R_QK, R_V, R_V)
    cuts = [sum(sizes[:i + 1]) for i in range(len(sizes) - 1)]
    dq, dk, dv, rq, rk, rv, rg = jnp.split(p, cuts, axis=-1)
    return (dq.reshape(bn, t, A_HEADS, 2, HEAD_DIM),
            dk.reshape(bn, t, A_HEADS, 2, HEAD_DIM),
            dv.reshape(bn, t, A_HEADS, 2 * HEAD_DIM),
            rq.reshape(bn, t, R_HEADS, R_DK),
            rk.reshape(bn, t, R_HEADS, R_DK),
            rv.reshape(bn, t, R_HEADS, R_DV),
            rg)

def diff_attend(q, k, v, lam):
    s = jnp.einsum('bqhmd,bkhmd->bhmqk', q, k).astype(jnp.float32)
    p = jax.nn.softmax(s, axis=-1)
    a = p[:, :, 0] - lam * p[:, :, 1]
    return jnp.einsum('bhqk,bkhe->bqhe', a.astype(v.dtype), v)

def retention_chunked(q, k, v, log_gamma, state0):
    b, t, h, dk = q.shape
    dv = v.shape[-1]
    n = t // RET_CHUNK
    f32 = jnp.float32
    qc = q.astype(f32).reshape(b, n, RET_CHUNK, h, dk)
    kc = k.astype(f32).reshape(b, n, RET_CHUNK, h, dk)
    vc = v.astype(f32).reshape(b, n, RET_CHUNK, h, dv)
    lg = log_gamma.astype(f32)
    pos = jnp.arange(RET_CHUNK, dtype=f32)
    rel = pos[:, None] - pos[None, :]
    decay = jnp.where(rel[None] >= 0, jnp.exp(jnp.maximum(rel, 0.0)[None] * lg[:, None, None]), 0.0)
    scores = jnp.einsum('bnihd,bnjhd->bnhij', qc, kc) * decay
    intra = jnp.einsum('bnhij,bnjhe->bnihe', scores, vc)
    k_dec = kc * jnp.exp((RET_CHUNK - 1 - pos)[:, None] * lg)[:, :, None]
    chunk_kv = jnp.einsum('bnjhd,bnjhe->nbhde', k_dec, vc)
    g_chunk = jnp.exp(RET_CHUNK * lg)[None, :, None, None]

    def step(s, kv_i):
        return g_chunk * s + kv_i, s

    state_final, state_prev = lax.scan(step, state0.astype(f32), chunk_kv)
    q_dec = qc * jnp.exp((pos + 1)[:, None] * lg)[:, :, None]
    cross = jnp.einsum('bnihd,nbhde->bnihe', q_dec, state_prev)
    out = (intra + cross).reshape(b, t, h, dv)
    return out.astype(v.dtype), state_final

def bidir_retention(q_c, k_c, v_c, q_x, k_x, v_x, logg_f, logg_b):
    b = q_x.shape[0]
    s0 = jnp.zeros((b, R_HEADS, R_DK, R_DV), jnp.float32)
    flip = lambda a: jnp.flip(a, axis=1)
    o_cf, s_cf = retention_chunked(q_c, k_c, v_c, logg_f, s0)
    o_xf, _ = retention_chunked(q_x, k_x, v_x, logg_f, s_cf)
    o_cb, s_cb = retention_chunked(flip(q_c), flip(k_c), flip(v_c), logg_b, s0)
    o_xb, _ = retention_chunked(flip(q_x), flip(k_x), flip(v_x), logg_b, s_cb)
    return o_cf + flip(o_cb), o_xf + flip(o_xb)

def mixer_merge(att, ret, gate, lam_init, dattn_norm_g, ret_norm_g, w_out):
    bn, t = att.shape[:2]
    a = (rmsnorm(att, dattn_norm_g) * (1 - lam_init)).reshape(bn, t, A_V)
    r = jax.nn.silu(gate) * rmsnorm(ret, ret_norm_g).reshape(bn, t, R_V)
    return jnp.concatenate([a, r], axis=-1) @ w_out

def moe_ffn(h, router_w, router_bias, w1, w3, w2, sw1, sw3, sw2):
    t, d = h.shape
    scores = jax.nn.sigmoid((h @ router_w).astype(jnp.float32))
    sel = scores + router_bias.astype(jnp.float32)
    grp = sel.reshape(t, N_GROUPS, N_EXPERTS // N_GROUPS)
    grp_score = lax.top_k(grp, 2)[0].sum(-1)
    _, top_g = lax.top_k(grp_score, TOPK_GROUPS)
    gmask = jax.nn.one_hot(top_g, N_GROUPS, dtype=jnp.float32).sum(axis=1) > 0
    emask = jnp.repeat(gmask, N_EXPERTS // N_GROUPS, axis=1)
    _, top_e = lax.top_k(jnp.where(emask, sel, -jnp.inf), TOP_K)
    wts = jnp.take_along_axis(scores, top_e, axis=1)
    wts = wts / jnp.sum(wts, axis=-1, keepdims=True) * ROUTED_SCALE
    n_assign = t * TOP_K
    e_flat = top_e.reshape(n_assign)
    t_flat = jnp.repeat(jnp.arange(t, dtype=jnp.int32), TOP_K)
    w_flat = wts.reshape(n_assign)
    order = jnp.argsort(e_flat)
    e_s, t_s, w_s = e_flat[order], t_flat[order], w_flat[order]
    counts = jax.ops.segment_sum(jnp.ones((n_assign,), jnp.int32), e_flat, num_segments=N_EXPERTS)
    padded = (counts + MOE_BLOCK - 1) // MOE_BLOCK * MOE_BLOCK
    pad_end = jnp.cumsum(padded)
    pad_start = pad_end - padded
    start = jnp.cumsum(counts) - counts
    dest = pad_start[e_s] + jnp.arange(n_assign, dtype=jnp.int32) - start[e_s]
    n_pad = -(-n_assign // MOE_BLOCK) * MOE_BLOCK + N_EXPERTS * MOE_BLOCK
    n_blk = n_pad // MOE_BLOCK
    tok_buf = jnp.full((n_pad,), t, jnp.int32).at[dest].set(t_s)
    w_buf = jnp.zeros((n_pad,), jnp.float32).at[dest].set(w_s)
    blk_exp = jnp.clip(jnp.searchsorted(pad_end, jnp.arange(n_blk, dtype=jnp.int32) * MOE_BLOCK, side='right'),
                       0, N_EXPERTS - 1).astype(jnp.int32)
    h_pad = jnp.concatenate([h, jnp.zeros((1, d), h.dtype)], axis=0)

    def body(acc, inp):
        tok, wt, e = inp
        xb = h_pad[tok]
        yb = (jax.nn.silu(xb @ w1[e]) * (xb @ w3[e])) @ w2[e]
        return acc.at[tok].add((yb * wt[:, None].astype(yb.dtype)).astype(acc.dtype)), None

    acc0 = jnp.zeros((t + 1, d), h.dtype)
    acc, _ = lax.scan(body, acc0, (tok_buf.reshape(n_blk, MOE_BLOCK), w_buf.reshape(n_blk, MOE_BLOCK), blk_exp))
    shared = (jax.nn.silu(h @ sw1) * (h @ sw3)) @ sw2
    return acc[:t] + shared

def hybrid_layer(x, xc, mod_x, mod_c, cos, sin, lam_init, update_ctx,
                 norm1_g, w_in, lambda_q1, lambda_k1, lambda_q2, lambda_k2, dattn_norm_g,
                 ret_decay_fwd, ret_decay_bwd, ret_norm_g, w_out,
                 norm2_g, router_w, router_bias, exp_w1, exp_w3, exp_w2,
                 shared_w1, shared_w3, shared_w2):
    b, s, d = x.shape
    sh1, sc1, g1, sh2, sc2, g2 = jnp.split(mod_x, 6, axis=-1)
    csh1, csc1, cg1, csh2, csc2, cg2 = jnp.split(mod_c, 6, axis=-1)

    hx = modulate(rmsnorm(x, norm1_g), sh1, sc1)
    hc = modulate(rmsnorm(xc, norm1_g), csh1, csc1)
    dq_x, dk_x, dv_x, rq_x, rk_x, rv_x, rg_x = project_heads(hx, w_in)
    dq_c, dk_c, dv_c, rq_c, rk_c, rv_c, rg_c = project_heads(hc, w_in)

    dq_x = apply_axial_rope(dq_x, cos, sin) * HEAD_DIM ** -0.5
    dk_x = apply_axial_rope(dk_x, cos, sin)
    rq_x = apply_axial_rope(rq_x, cos, sin)
    rk_x = apply_axial_rope(rk_x, cos, sin) * R_DK ** -0.5
    dq_c = dq_c * HEAD_DIM ** -0.5
    rk_c = rk_c * R_DK ** -0.5

    lam = (jnp.exp(jnp.sum(lambda_q1 * lambda_k1)) - jnp.exp(jnp.sum(lambda_q2 * lambda_k2))).astype(jnp.float32) + lam_init

    k_all = jnp.concatenate([dk_c, dk_x], axis=1)
    v_all = jnp.concatenate([dv_c, dv_x], axis=1)
    n_qblk = s // Q_BLOCK
    q_blocks = dq_x.reshape(b, n_qblk, Q_BLOCK, A_HEADS, 2, HEAD_DIM).swapaxes(0, 1)
    att_x = lax.map(lambda qb: diff_attend(qb, k_all, v_all, lam), q_blocks)
    att_x = att_x.swapaxes(0, 1).reshape(b, s, A_HEADS, 2 * HEAD_DIM)

    logg_f = jax.nn.log_sigmoid(ret_decay_fwd.astype(jnp.float32))
    logg_b = jax.nn.log_sigmoid(ret_decay_bwd.astype(jnp.float32))
    ret_c, ret_x = bidir_retention(rq_c, rk_c, rv_c, rq_x, rk_x, rv_x, logg_f, logg_b)

    y_x = mixer_merge(att_x, ret_x, rg_x, lam_init, dattn_norm_g, ret_norm_g, w_out)
    x = x + g1[:, None] * y_x
    h2 = modulate(rmsnorm(x, norm2_g), sh2, sc2)
    ffn_x = moe_ffn(h2.reshape(b * s, d), router_w, router_bias, exp_w1, exp_w3, exp_w2,
                    shared_w1, shared_w3, shared_w2).reshape(b, s, d)
    x = x + g2[:, None] * ffn_x

    if update_ctx:
        att_c = diff_attend(dq_c, dk_c, dv_c, lam)
        y_c = mixer_merge(att_c, ret_c, rg_c, lam_init, dattn_norm_g, ret_norm_g, w_out)
        xc = xc + cg1[:, None] * y_c
        bc, lc, _ = xc.shape
        h2c = modulate(rmsnorm(xc, norm2_g), csh2, csc2)
        ffn_c = moe_ffn(h2c.reshape(bc * lc, d), router_w, router_bias, exp_w1, exp_w3, exp_w2,
                        shared_w1, shared_w3, shared_w2).reshape(bc, lc, d)
        xc = xc + cg2[:, None] * ffn_c
    else:
        xc = None
    return x, xc

def first_inputs(seed: int = 0) -> dict:
    key = jax.random.key(seed)
    ks = jax.random.split(key, 32)
    f32 = jnp.float32

    def nrm(k, shape, scale):
        return jax.random.normal(k, shape, f32) * scale

    gamma0 = 1.0 - 2.0 ** (-5.0 - jnp.arange(R_HEADS, dtype=f32))
    logit0 = jnp.log(gamma0) - jnp.log1p(-gamma0)
    return {
        "x": nrm(ks[0], (BATCH, SEQ, D_MODEL), 1.0),
        "c": nrm(ks[1], (BATCH, D_MODEL), 1.0),
        "ctx": nrm(ks[2], (BATCH, CTX_LEN, D_MODEL), 1.0),
        "c_ctx": nrm(ks[3], (D_MODEL,), 1.0),
        "ada_w": nrm(ks[4], (DEPTH, D_MODEL, 6 * D_MODEL), 0.5 * D_MODEL ** -0.5),
        "ada_b": nrm(ks[5], (DEPTH, 6 * D_MODEL), 0.02),
        "norm1_g": 1.0 + nrm(ks[6], (DEPTH, D_MODEL), 0.05),
        "w_in": nrm(ks[7], (DEPTH, D_MODEL, D_IN), D_MODEL ** -0.5),
        "lambda_q1": nrm(ks[8], (DEPTH, HEAD_DIM), 0.1),
        "lambda_k1": nrm(ks[9], (DEPTH, HEAD_DIM), 0.1),
        "lambda_q2": nrm(ks[10], (DEPTH, HEAD_DIM), 0.1),
        "lambda_k2": nrm(ks[11], (DEPTH, HEAD_DIM), 0.1),
        "dattn_norm_g": 1.0 + nrm(ks[12], (DEPTH, 2 * HEAD_DIM), 0.05),
        "ret_decay_fwd": logit0[None] + nrm(ks[13], (DEPTH, R_HEADS), 0.1),
        "ret_decay_bwd": logit0[None] + nrm(ks[14], (DEPTH, R_HEADS), 0.1),
        "ret_norm_g": 1.0 + nrm(ks[15], (DEPTH, R_DV), 0.05),
        "w_out": nrm(ks[16], (DEPTH, D_MIX, D_MODEL), D_MIX ** -0.5),
        "norm2_g": 1.0 + nrm(ks[17], (DEPTH, D_MODEL), 0.05),
        "router_w": nrm(ks[18], (DEPTH, D_MODEL, N_EXPERTS), D_MODEL ** -0.5),
        "router_bias": nrm(ks[19], (DEPTH, N_EXPERTS), 0.01),
        "exp_w1": nrm(ks[20], (DEPTH, N_EXPERTS, D_MODEL, D_EXPERT), D_MODEL ** -0.5),
        "exp_w3": nrm(ks[21], (DEPTH, N_EXPERTS, D_MODEL, D_EXPERT), D_MODEL ** -0.5),
        "exp_w2": nrm(ks[22], (DEPTH, N_EXPERTS, D_EXPERT, D_MODEL), D_EXPERT ** -0.5),
        "shared_w1": nrm(ks[23], (DEPTH, D_MODEL, D_SHARED), D_MODEL ** -0.5),
        "shared_w3": nrm(ks[24], (DEPTH, D_MODEL, D_SHARED), D_MODEL ** -0.5),
        "shared_w2": nrm(ks[25], (DEPTH, D_SHARED, D_MODEL), D_SHARED ** -0.5),
        "final_norm_g": 1.0 + nrm(ks[26], (D_MODEL,), 0.05),
    }

def first_block(x, c, ctx, c_ctx, ada_w, ada_b, norm1_g, w_in, lambda_q1, lambda_k1, lambda_q2, lambda_k2,
              dattn_norm_g, ret_decay_fwd, ret_decay_bwd, ret_norm_g, w_out, norm2_g, router_w, router_bias,
              exp_w1, exp_w3, exp_w2, shared_w1, shared_w3, shared_w2, final_norm_g):
    s = x.shape[1]
    cos, sin = axial_rope_tables(s)
    xc = ctx
    for l in range(DEPTH):
        lam_init = 0.8 - 0.6 * math.exp(-0.3 * l)
        mod_x = jax.nn.silu(c) @ ada_w[l] + ada_b[l]
        mod_c = (jax.nn.silu(c_ctx) @ ada_w[l] + ada_b[l])[None]
        x, xc = hybrid_layer(x, xc, mod_x, mod_c, cos, sin, lam_init, l < DEPTH - 1,
                             norm1_g[l], w_in[l], lambda_q1[l], lambda_k1[l], lambda_q2[l], lambda_k2[l],
                             dattn_norm_g[l], ret_decay_fwd[l], ret_decay_bwd[l], ret_norm_g[l], w_out[l],
                             norm2_g[l], router_w[l], router_bias[l], exp_w1[l], exp_w3[l], exp_w2[l],
                             shared_w1[l], shared_w3[l], shared_w2[l])
    return rmsnorm(x, final_norm_g)


DEPTH_2 = 2

CHUNK = 64
N_EVEN = (DEPTH_2 + 1) // 2
N_ODD = DEPTH_2 // 2
DEEPNORM_ALPHA = (2.0 * DEPTH_2) ** 0.25
DEEPNORM_BETA = (8.0 * DEPTH_2) ** -0.25
D_FF = 2816
N_SUB = 3
LN_EPS = 1e-5
RMS_EPS = 1e-6
NEG_INF = -1e30

A_HEADS_2 = 8
A_HEAD_DIM = 64
A_WIDTH = A_HEADS_2 * A_HEAD_DIM
IDX_HEADS = 8
IDX_DIM = 64
TOPK_MAX = 256
SPARSE_Q_BLOCK = 32

B_HEADS = 4
B_HEAD_DIM = 128
B_WIDTH = B_HEADS * B_HEAD_DIM
CONV_K = 4

EVEN_SIZES = (A_WIDTH, A_WIDTH, A_WIDTH, IDX_HEADS * IDX_DIM, IDX_DIM, IDX_HEADS,
              3 * B_WIDTH, B_HEADS, B_HEADS, B_WIDTH)
EVEN_IN = sum(EVEN_SIZES)
EVEN_SPLITS = tuple(int(s) for s in np.cumsum(EVEN_SIZES)[:-1])
EVEN_MIX = A_WIDTH + B_WIDTH

C_HEADS = 16
C_Q_RANK = 384
C_KV_RANK = 256
C_NOPE = 64
C_ROPE = 32
C_V = 64
C_IN = C_Q_RANK + C_KV_RANK + C_ROPE
C_MIX = C_HEADS * C_V
ROPE_THETA = 10000.0
DENSE_Q_BLOCK = 128


def layer_norm(x, g, b):
    xf = x.astype(jnp.float32)
    mu = jnp.mean(xf, -1, keepdims=True)
    var = jnp.mean(jnp.square(xf - mu), -1, keepdims=True)
    return ((xf - mu) * lax.rsqrt(var + LN_EPS)).astype(x.dtype) * g + b

def rms_norm(x, g):
    xf = x.astype(jnp.float32)
    return (xf * lax.rsqrt(jnp.mean(xf * xf, -1, keepdims=True) + RMS_EPS)).astype(x.dtype) * g

def l2_normalize(x):
    return x * lax.rsqrt(jnp.sum(x * x, -1, keepdims=True) + RMS_EPS)

def swiglu(u, w_gate, w_up, w_down):
    return (jax.nn.silu(u @ w_gate) * (u @ w_up)) @ w_down

def alibi_slopes(n):
    return jnp.asarray(2.0 ** (-8.0 * np.arange(1, n + 1) / n), dtype=jnp.float32)

def rope(x, pos):
    half = x.shape[-1] // 2
    inv_freq = ROPE_THETA ** (-jnp.arange(half, dtype=jnp.float32) / half)
    ang = pos.astype(jnp.float32)[:, :, None] * inv_freq
    cos, sin = jnp.cos(ang)[:, :, None, :], jnp.sin(ang)[:, :, None, :]
    xf = x.astype(jnp.float32)
    x1, x2 = xf[..., :half], xf[..., half:]
    return jnp.concatenate([x1 * cos - x2 * sin, x1 * sin + x2 * cos], -1).astype(x.dtype)

def to_query_blocks(t, size):
    return t.reshape(t.shape[0], t.shape[1] // size, size, *t.shape[2:]).swapaxes(0, 1)

def from_query_blocks(t):
    t = t.swapaxes(0, 1)
    return t.reshape(t.shape[0], t.shape[1] * t.shape[2], -1)

def dsa_attention(q, k, v, iq, ik, iw, pos):
    top_k = min(TOPK_MAX, pos.shape[1] // 4)
    key_chunk = pos // CHUNK
    slopes = alibi_slopes(A_HEADS_2)
    ik32 = ik.astype(jnp.float32)
    iw32 = iw.astype(jnp.float32) * IDX_HEADS ** -0.5
    gather = jax.vmap(lambda table, idx: table[idx])

    def block(args):
        qb, iqb, iwb, pb = args
        qchunk = pb // CHUNK
        dots = jnp.einsum('bqhd,bsd->bqhs', iqb.astype(jnp.float32), ik32) * IDX_DIM ** -0.5
        score = jnp.einsum('bqh,bqhs->bqs', iwb, jax.nn.relu(dots))
        visible = key_chunk[:, None, :] <= qchunk[:, :, None]
        score = jnp.where(visible, score, NEG_INF)
        _, sel = lax.top_k(score, top_k)
        k_sel = gather(k, sel)
        v_sel = gather(v, sel)
        pos_sel = gather(pos, sel)
        valid = (pos_sel // CHUNK) <= qchunk[:, :, None]
        dist = jnp.abs(pb[:, :, None] - pos_sel).astype(jnp.float32)
        logits = jnp.einsum('bqhd,bqkhd->bhqk', qb, k_sel,
                            preferred_element_type=jnp.float32) * A_HEAD_DIM ** -0.5
        logits = logits - slopes[None, :, None, None] * dist[:, None]
        p = jax.nn.softmax(jnp.where(valid[:, None], logits, NEG_INF), axis=-1)
        return jnp.einsum('bhqk,bqkhd->bqhd', p.astype(v.dtype), v_sel)

    out = lax.map(block, (to_query_blocks(q, SPARSE_Q_BLOCK), to_query_blocks(iq, SPARSE_Q_BLOCK),
                          to_query_blocks(iw32, SPARSE_Q_BLOCK), to_query_blocks(pos, SPARSE_Q_BLOCK)))
    return from_query_blocks(out)

def causal_depthwise_conv(x, w):
    return lax.conv_general_dilated(x, w[:, None, :].astype(x.dtype), window_strides=(1,),
                                    padding=[(CONV_K - 1, 0)],
                                    dimension_numbers=('NWC', 'WIO', 'NWC'),
                                    feature_group_count=x.shape[-1])

def gated_delta_rule(q, k, v, g, beta):
    bsz, seq, nh, dk = q.shape
    n = seq // CHUNK

    def to_chunks(t):
        t = t.reshape(bsz, n, CHUNK, nh, *t.shape[3:])
        return jnp.moveaxis(t, (1, 3), (0, 2))

    qc = to_chunks(q * dk ** -0.5)
    kc, vc, bc = to_chunks(k), to_chunks(v), to_chunks(beta)
    gc = jnp.cumsum(to_chunks(g), axis=-1)
    incl = jnp.tril(jnp.ones((CHUNK, CHUNK), dtype=bool))
    strict = jnp.tril(jnp.ones((CHUNK, CHUNK), dtype=bool), -1)
    decay = jnp.exp(jnp.where(incl, gc[..., :, None] - gc[..., None, :], -jnp.inf))
    kb = kc * bc[..., None]
    vb = vc * bc[..., None]
    m = jnp.where(strict, jnp.einsum('nbhid,nbhjd->nbhij', kb, kc) * decay, 0.0)
    eye = jnp.eye(CHUNK, dtype=jnp.float32)
    t_inv = lax.linalg.triangular_solve(eye + m, jnp.broadcast_to(eye, m.shape), left_side=True,
                                        lower=True, unit_diagonal=True)
    u = t_inv @ vb
    w = t_inv @ (kb * jnp.exp(gc)[..., None])
    attn_intra = jnp.where(incl, jnp.einsum('nbhid,nbhjd->nbhij', qc, kc) * decay, 0.0)

    def step(state, xs):
        q_i, k_i, u_i, w_i, g_i, a_i = xs
        v_new = u_i - w_i @ state
        o = (q_i * jnp.exp(g_i)[..., None]) @ state + a_i @ v_new
        g_last = g_i[..., -1]
        k_dec = k_i * jnp.exp(g_last[..., None] - g_i)[..., None]
        state = state * jnp.exp(g_last)[..., None, None] + jnp.einsum('bhcd,bhce->bhde', k_dec, v_new)
        return state, o

    s0 = jnp.zeros((bsz, nh, dk, v.shape[-1]), jnp.float32)
    _, o = lax.scan(step, s0, (qc, kc, u, w, gc, attn_intra))
    return jnp.moveaxis(o, (0, 2), (1, 3)).reshape(bsz, seq, nh, v.shape[-1])

def gdn_mixer(qkv, a, b, z, conv_w, a_log, dt_bias, norm_g):
    bsz, seq, _ = qkv.shape
    qkv = jax.nn.silu(causal_depthwise_conv(qkv, conv_w))
    q, k, v = jnp.split(qkv.astype(jnp.float32), 3, axis=-1)
    q = l2_normalize(q.reshape(bsz, seq, B_HEADS, B_HEAD_DIM))
    k = l2_normalize(k.reshape(bsz, seq, B_HEADS, B_HEAD_DIM))
    v = v.reshape(bsz, seq, B_HEADS, B_HEAD_DIM)
    g = -jnp.exp(a_log.astype(jnp.float32)) * jax.nn.softplus(a.astype(jnp.float32) + dt_bias.astype(jnp.float32))
    beta = jax.nn.sigmoid(b.astype(jnp.float32))
    o = gated_delta_rule(q, k, v, g, beta).astype(z.dtype)
    o = rms_norm(o, norm_g) * jax.nn.silu(z.reshape(bsz, seq, B_HEADS, B_HEAD_DIM))
    return o.reshape(bsz, seq, B_WIDTH)

def hybrid_mixer(u, pos, w_in, w_out, conv_w, a_log, dt_bias, norm_g):
    bsz, seq, _ = u.shape
    a_q, a_k, a_v, i_q, i_k, i_w, b_qkv, b_a, b_b, b_z = jnp.split(u @ w_in, EVEN_SPLITS, axis=-1)
    heads = lambda t, nh: t.reshape(bsz, seq, nh, -1)
    out_a = dsa_attention(heads(a_q, A_HEADS_2), heads(a_k, A_HEADS_2), heads(a_v, A_HEADS_2),
                          heads(i_q, IDX_HEADS), i_k, i_w, pos)
    out_b = gdn_mixer(b_qkv, b_a, b_b, b_z, conv_w, a_log, dt_bias, norm_g)
    return jnp.concatenate([out_a.astype(u.dtype), out_b], axis=-1) @ w_out

def chunk_causal_attention(q, k, v, pos, scale):
    key_chunk = pos // CHUNK

    def block(args):
        qb, pb = args
        logits = jnp.einsum('bqhd,bshd->bhqs', qb, k, preferred_element_type=jnp.float32) * scale
        visible = key_chunk[:, None, None, :] <= (pb // CHUNK)[:, None, :, None]
        p = jax.nn.softmax(jnp.where(visible, logits, NEG_INF), axis=-1)
        return jnp.einsum('bhqs,bshd->bqhd', p.astype(v.dtype), v)

    out = lax.map(block, (to_query_blocks(q, DENSE_Q_BLOCK), to_query_blocks(pos, DENSE_Q_BLOCK)))
    return from_query_blocks(out)

def mla_mixer(u, pos, w_in, q_norm_g, w_q_up, kv_norm_g, w_kv_up, w_out):
    bsz, seq, _ = u.shape
    c_q, c_kv, k_rope = jnp.split(u @ w_in, [C_Q_RANK, C_Q_RANK + C_KV_RANK], axis=-1)
    q = (rms_norm(c_q, q_norm_g) @ w_q_up).reshape(bsz, seq, C_HEADS, C_NOPE + C_ROPE)
    kv = (rms_norm(c_kv, kv_norm_g) @ w_kv_up).reshape(bsz, seq, C_HEADS, C_NOPE + C_V)
    q = jnp.concatenate([q[..., :C_NOPE], rope(q[..., C_NOPE:], pos)], axis=-1)
    k_rope = jnp.broadcast_to(rope(k_rope[:, :, None, :], pos), (bsz, seq, C_HEADS, C_ROPE))
    k = jnp.concatenate([kv[..., :C_NOPE], k_rope], axis=-1)
    v = kv[..., C_NOPE:]
    out = chunk_causal_attention(q, k, v, pos, (C_NOPE + C_ROPE) ** -0.5)
    return out @ w_out

def adaln_sublayer(x, m, f, ln_g, ln_b):
    shift, scale, gate = m[:, None, 0], m[:, None, 1], m[:, None, 2]
    y = f(x * (1 + scale) + shift)
    return layer_norm(DEEPNORM_ALPHA * x + (1 + gate) * y, ln_g, ln_b)

def second_inputs(seed: int = 0) -> dict:
    key = jax.random.key(seed)
    ks = iter(jax.random.split(key, 32))

    def nrm(shape, fan_in, s=1.0):
        return jax.random.normal(next(ks), shape, jnp.float32) * (s * fan_in ** -0.5)

    def gain(shape):
        return 1.0 + 0.02 * jax.random.normal(next(ks), shape, jnp.float32)

    def small(shape, s=0.02):
        return s * jax.random.normal(next(ks), shape, jnp.float32)

    x = jax.random.normal(next(ks), (BATCH, SEQ, D_MODEL), jnp.float32)
    c = jax.random.normal(next(ks), (BATCH, D_MODEL), jnp.float32)
    offsets = jax.random.randint(next(ks), (BATCH, 1), 0, 1024) * CHUNK
    positions = (offsets + jnp.arange(SEQ)[None, :]).astype(jnp.int32)
    dt = jnp.exp(jax.random.uniform(next(ks), (N_EVEN, B_HEADS), jnp.float32,
                                    math.log(1e-3), math.log(1e-1)))
    return {
        "x": x,
        "c": c,
        "positions": positions,
        "mod_w": nrm((DEPTH_2, D_MODEL, N_SUB * 3 * D_MODEL), D_MODEL, 0.1),
        "mod_b": small((DEPTH_2, N_SUB * 3 * D_MODEL), 0.01),
        "ln_g": gain((DEPTH_2, N_SUB, D_MODEL)),
        "ln_b": small((DEPTH_2, N_SUB, D_MODEL)),
        "ffn_w_gate": nrm((DEPTH_2, 2, D_MODEL, D_FF), D_MODEL),
        "ffn_w_up": nrm((DEPTH_2, 2, D_MODEL, D_FF), D_MODEL),
        "ffn_w_down": nrm((DEPTH_2, 2, D_FF, D_MODEL), D_FF, DEEPNORM_BETA),
        "hyb_w_in": nrm((N_EVEN, D_MODEL, EVEN_IN), D_MODEL),
        "hyb_w_out": nrm((N_EVEN, EVEN_MIX, D_MODEL), EVEN_MIX, DEEPNORM_BETA),
        "gdn_conv_w": nrm((N_EVEN, CONV_K, 3 * B_WIDTH), CONV_K),
        "gdn_a_log": jnp.log(jax.random.uniform(next(ks), (N_EVEN, B_HEADS), jnp.float32, 1.0, 16.0)),
        "gdn_dt_bias": dt + jnp.log(-jnp.expm1(-dt)),
        "gdn_norm_g": gain((N_EVEN, B_HEAD_DIM)),
        "mla_w_in": nrm((N_ODD, D_MODEL, C_IN), D_MODEL),
        "mla_q_norm_g": gain((N_ODD, C_Q_RANK)),
        "mla_w_q_up": nrm((N_ODD, C_Q_RANK, C_HEADS * (C_NOPE + C_ROPE)), C_Q_RANK),
        "mla_kv_norm_g": gain((N_ODD, C_KV_RANK)),
        "mla_w_kv_up": nrm((N_ODD, C_KV_RANK, C_HEADS * (C_NOPE + C_V)), C_KV_RANK),
        "mla_w_out": nrm((N_ODD, C_MIX, D_MODEL), C_MIX, DEEPNORM_BETA),
    }

def second_block(x, c, positions, mod_w, mod_b, ln_g, ln_b, ffn_w_gate, ffn_w_up, ffn_w_down,
              hyb_w_in, hyb_w_out, gdn_conv_w, gdn_a_log, gdn_dt_bias, gdn_norm_g,
              mla_w_in, mla_q_norm_g, mla_w_q_up, mla_kv_norm_g, mla_w_kv_up, mla_w_out):
    bsz = x.shape[0]
    cs = jax.nn.silu(c)
    for layer in range(DEPTH_2):
        mod = (cs @ mod_w[layer] + mod_b[layer]).reshape(bsz, N_SUB, 3, D_MODEL)
        x = adaln_sublayer(x, mod[:, 0], lambda u: 0.5 * swiglu(u, ffn_w_gate[layer, 0], ffn_w_up[layer, 0],
                                                               ffn_w_down[layer, 0]),
                           ln_g[layer, 0], ln_b[layer, 0])
        if layer % 2 == 0:
            e = layer // 2
            x = adaln_sublayer(x, mod[:, 1], lambda u: hybrid_mixer(u, positions, hyb_w_in[e], hyb_w_out[e],
                                                                    gdn_conv_w[e], gdn_a_log[e],
                                                                    gdn_dt_bias[e], gdn_norm_g[e]),
                               ln_g[layer, 1], ln_b[layer, 1])
        else:
            o = layer // 2
            x = adaln_sublayer(x, mod[:, 1], lambda u: mla_mixer(u, positions, mla_w_in[o], mla_q_norm_g[o],
                                                                 mla_w_q_up[o], mla_kv_norm_g[o],
                                                                 mla_w_kv_up[o], mla_w_out[o]),
                               ln_g[layer, 1], ln_b[layer, 1])
        x = adaln_sublayer(x, mod[:, 2], lambda u: 0.5 * swiglu(u, ffn_w_gate[layer, 1], ffn_w_up[layer, 1],
                                                               ffn_w_down[layer, 1]),
                           ln_g[layer, 2], ln_b[layer, 2])
    return x


def setup_inputs(seed=0):
    out = dict(first_inputs(seed))
    for name, value in second_inputs(seed + 1).items():
        if name != "x":
            out[name + "_2"] = value
    return out


def reference(
    x, c, ctx, c_ctx, ada_w, ada_b, norm1_g, w_in, lambda_q1, lambda_k1, lambda_q2, lambda_k2,
    dattn_norm_g, ret_decay_fwd, ret_decay_bwd, ret_norm_g, w_out, norm2_g, router_w,
    router_bias, exp_w1, exp_w3, exp_w2, shared_w1, shared_w3, shared_w2, final_norm_g, c_2,
    positions_2, mod_w_2, mod_b_2, ln_g_2, ln_b_2, ffn_w_gate_2, ffn_w_up_2, ffn_w_down_2,
    hyb_w_in_2, hyb_w_out_2, gdn_conv_w_2, gdn_a_log_2, gdn_dt_bias_2, gdn_norm_g_2, mla_w_in_2,
    mla_q_norm_g_2, mla_w_q_up_2, mla_kv_norm_g_2, mla_w_kv_up_2, mla_w_out_2,
):
    x = first_block(
        x, c, ctx, c_ctx, ada_w, ada_b, norm1_g, w_in, lambda_q1, lambda_k1, lambda_q2,
        lambda_k2, dattn_norm_g, ret_decay_fwd, ret_decay_bwd, ret_norm_g, w_out, norm2_g,
        router_w, router_bias, exp_w1, exp_w3, exp_w2, shared_w1, shared_w3, shared_w2,
        final_norm_g,
    )
    return second_block(
        x, c_2, positions_2, mod_w_2, mod_b_2, ln_g_2, ln_b_2, ffn_w_gate_2, ffn_w_up_2,
        ffn_w_down_2, hyb_w_in_2, hyb_w_out_2, gdn_conv_w_2, gdn_a_log_2, gdn_dt_bias_2,
        gdn_norm_g_2, mla_w_in_2, mla_q_norm_g_2, mla_w_q_up_2, mla_kv_norm_g_2, mla_w_kv_up_2,
        mla_w_out_2,
    )


_drawn_inputs = setup_inputs


def setup_inputs(seed=0):
    import zlib

    import numpy as np

    out = dict(_drawn_inputs(seed))
    spreads = {}
    factors = {'lambda_k1': 8.0,
     'lambda_q2': 8.0,
     'mod_b_2': 3.779,
     'gdn_a_log_2': 8.0,
     'gdn_dt_bias_2': 2.959,
     'gdn_norm_g_2': 8.0,
     'mla_q_norm_g_2': 8.0,
     'mla_kv_norm_g_2': 8.0}
    for name, (base, spread) in spreads.items():
        noise = np.random.default_rng([zlib.crc32(name.encode()), seed]).standard_normal(out[name].shape)
        drawn = base * np.exp(spread * noise) if base else spread * noise
        out[name] = __import__('jax').numpy.asarray(drawn.astype(out[name].dtype))
    for name, factor in factors.items():
        out[name] = (out[name] * factor).astype(out[name].dtype)
    return out
```

```python
import math
from contextlib import ExitStack

import numpy as np

import concourse.bass as bass
from concourse import mybir


P = 128
D = 1024
KT = D // P
T = 256
TT = T // P
HALF = 256
N_EXP = 64
D_EXP = 256
D_FF = 2816
SLOTS = 6
SLOT = KT * HALF
DH = 64
A_HEADS = 4
R_HEADS = 4
IDX_HEADS = 8
B_HEADS = 4
C_HEADS = 16
C_QK = 96
TOPK = 64
ALPHA = (2.0 * 2) ** 0.25
EVEN_IN = 4176
NORM_EPS = 1e-6
LN_EPS = 1e-5
NEG = -1e30
TAKEN = -3e38

MOE_UNITS = N_EXP + 1
FFN_UNITS = D_FF // HALF
PHASES = [("moe", MOE_UNITS), ("ffn0", FFN_UNITS), ("ffn1", FFN_UNITS), ("ffn2", FFN_UNITS), ("ffn3", FFN_UNITS)]
PEELED = 3
MOD_SLOTS = 36
ADA_LATE = 16

PARAMS = {}
_at = 0
for _name, _n in [("norm1_g", 8), ("norm2_g", 8), ("final_g", 8), ("c", 8), ("c_ctx", 8), ("c2", 8),
                  ("ada_b", 48), ("dattn_g", 1), ("ret_g", 1), ("gdn_g", 1), ("q_g", 3), ("kv_g", 2),
                  ("ln_g", 48), ("ln_b", 48),
                  ("mod_b0", 72), ("conv", 48),
                  ("mod_b1", 72)]:
    PARAMS[_name] = (_at, _n)
    _at += _n
PARAM_TILES = [(0, 104), (104, 200), (200, 320), (320, 392)]


def shape_constants():
    p = np.arange(P)
    ident = np.eye(P, dtype=np.float32)
    ones = np.ones((P, P), np.float32)
    t = np.arange(T)
    inv = (np.float32(10000.0) ** (-np.arange(16, dtype=np.float32) / np.float32(16))).astype(np.float32)
    d = p % 64
    axis, half, f = d // 32, (d % 32) // 16, d % 16
    pos = np.where(axis[:, None] == 0, (t // 64)[None, :], (t % 64)[None, :]).astype(np.float32)
    ang = (pos * inv[f][:, None]).astype(np.float32).astype(np.float64)
    cos, sin = np.cos(ang).astype(np.float32), np.sin(ang).astype(np.float32)
    swap = np.zeros((P, P), np.float32)
    for q in range(P):
        if half[q] == 0:
            swap[q + 16, q] = -1.0
        else:
            swap[q - 16, q] = 1.0
    always = np.concatenate([ident, ones, cos, sin, swap], axis=1)
    i = np.arange(T)[None, :]
    fwd, bwd = [], []
    for kt in range(2):
        j = (kt * P + p)[:, None]
        fwd.append(T + i - j)
        bwd.append(T - i + j)
    for kt in range(2):
        j = (kt * P + p)[:, None]
        fwd.append(abs(i - j))
        bwd.append(abs(i - j))
    mf = [(i >= (kt * P + p)[:, None]) for kt in range(2)]
    mb = [(i <= (kt * P + p)[:, None]) for kt in range(2)]
    dist = np.concatenate(fwd + bwd, axis=1).astype(np.float32)
    dirs = np.concatenate(mf + mb, axis=1).astype(np.float32)
    jj, ii = p[:, None], p[None, :]
    levels = []
    b = 1
    while b < P:
        levels.append((jj // (2 * b) == ii // (2 * b)) & (ii % (2 * b) >= b) & (jj % (2 * b) < b))
        b *= 2
    chunk = np.concatenate(levels + [ii >= jj, ii > jj], axis=1).astype(np.float32)
    rot = np.zeros((P, C_QK + 1), np.float32)
    for q in range(16):
        rot[64 + 16 + q, 64 + q] = -1.0
        rot[64 + q, 64 + 16 + q] = 1.0
        rot[64 + q, C_QK] = inv[q]
        rot[80 + q, C_QK] = inv[q]
    heads = np.zeros((4, 4 * P), np.float32)
    for h in range(4):
        heads[h, h * P:(h + 1) * P] = 1.0
    return {"k_heads": heads, "k_always": always, "k_dist": dist, "k_dirs": dirs, "k_chunk": chunk, "k_rot": rot}


def build(nc, A, out, route_rows):
    F32 = mybir.dt.float32
    I32 = mybir.dt.int32
    ALU = mybir.AluOpType
    ACT = mybir.ActivationFunctionType
    AX = mybir.AxisListType.X
    ctx = ExitStack()
    with ctx:
        sems = {}

        def S(name):
            if name not in sems:
                sems[name] = ctx.enter_context(nc.semaphore(name))
            return sems[name]

        def sb(name, shape, dt=F32):
            return ctx.enter_context(nc.sbuf_tensor(name, shape, dt))

        WR = sb("weight_ring", [P, SLOTS, SLOT])
        MR = sb("mod_ring", [P, 2, SLOT])
        ARENA = sb("arena", [P, 2 * MOD_SLOTS * HALF])
        XS = sb("x_streams", [P, 2, KT, T])
        H = sb("h", [P, KT, 2 * T])
        SQ = sb("squares", [P, KT, T])
        HID = sb("hidden", [P, 2, 2, T])
        SIL = sb("silu_gate", [P, 2, 2, T])
        GW = sb("expert_weight", [P, 2, T])
        RR = sb("rinv", [P, 2 * T])
        MEAN = sb("mean", [P, T])
        K0 = sb("always", [P, 896])
        COLS = sb("param_cols", [P, 392])
        MODC = sb("mod_cols", [P, 2, 72])
        MODA = sb("ada_cols", [P, 32])
        MODE = sb("ada_cols_early", [P, 16, 2])
        CS = sb("silu_c", [P, 3, KT])
        RW = sb("router_w", [P, KT, N_EXP])
        BC = sb("broadcast_params", [P, 512])
        SM = sb("small", [P, 256])
        AACC = sb("ada_acc", [P, 4, HALF])
        PS = ctx.enter_context(nc.psum_tensor("ps", [P, 8, 512], F32))

        IDN, ONES = K0[:, 0:128], K0[:, 128:256]
        COS, SIN, SWP = K0[:, 256:512], K0[:, 512:768], K0[:, 768:896]
        AXS = XS[:, 0]
        X = XS[:, 1]
        MIX = H[:, :, T:2 * T]
        U_IN = H[:, :, 0:T]

        def ar(off, *shape):
            n = int(np.prod(shape))
            v = ARENA[:, off:off + n]
            if len(shape) == 2:
                v = v.rearrange("p (a b) -> p a b", a=shape[0])
            if len(shape) == 3:
                v = v.rearrange("p (a b c) -> p a b c", a=shape[0], b=shape[1])
            return v

        def col(name, i=0, n=1):
            a = PARAMS[name][0] + i
            return COLS[:, a:a + n]

        def small(at, n=1):
            return SM[:, at:at + n]

        class Use:
            pass

        last_use = [None] * 8
        uses = {}

        def take(name, bank, full=None, free=None):
            u = Use()
            u.bank, u.prev = bank, last_use[bank]
            u.full = full or ("full", bank)
            u.free = free or ("free", bank)
            last_use[bank] = u
            uses[name] = u
            return u

        counts = {}

        def settle(u):
            if u.full[0] == "full":
                k = ("full", u.bank)
                counts[k] = counts.get(k, 0) + 1
                u.full = (f"bank{u.bank}_full", counts[k])
            if u.free[0] == "free":
                k = ("free", u.bank)
                counts[k] = counts.get(k, 0) + 1
                u.free = (f"bank{u.bank}_free", counts[k])
            return u

        def plan(name, bank, full=None, free=None):
            return settle(take(name, bank, full, free))

        loads = []
        released = []

        def load(view, width, rel):
            loads.append((view, width))
            released.append(rel)

        rows = lambda w: w.rearrange("(k p) n -> p k n", p=P)

        for n in range(8):
            plan(f"xt{n}", n % 4, free=(("xt_by_vector", "xt_by_scalar")[n % 2], n // 2 + 1))
        plan("params", 4, free=("cols_ready", 1))
        ada_v = rows(A["ada_w"][0])
        for n in range(4):
            plan(f"ada_row{n}", 6 + n % 2, full=("ada_slot_done", 2 * n + 2), free=("ada_row_copied", n + 1))
        for n in range(8):
            load(ada_v[:, :, n * HALF:(n + 1) * HALF], HALF, ("ada_slot_done", n + 1))
        plan("ms_first", 5)
        plan("ada_col", 5)
        w_in = rows(A["w_in"][0])
        for j in range(12):
            plan(f"pj{j}", j % 3, free=("raw_ready", j + 1))
            plan(f"sw{j}", 3 + j % 2)
        plan("ada_late", 7)
        for n in range(8):
            plan(f"vt{n}", 5 + n % 2, free=("values_copied", n + 1))
        for n in range(2):
            plan(f"rg{n}", n)
        col0 = {"dq": 0, "dk": 512, "dv": 1024, "rq": 1536, "rk": 1792, "rv": 2048, "rg": 2560}
        slot_cols = [0, 256, 512, 768, 1536, 1792, 1024, 1280, 2048, 2304, 2560, 2816]
        for n, c0 in enumerate(slot_cols):
            if n < 6:
                rel = uses[f"pj{2 * n + 1}"].full
            elif n < 10:
                rel = uses[f"vt{2 * (n - 6) + 1}"].full
            else:
                rel = uses[f"rg{n - 10}"].full
            load(w_in[:, :, c0:c0 + HALF], HALF, rel)
        L_ADA, L_PROJ = 0, 8
        for u in range(8):
            plan(f"ds{u}a", (2 * u) % 4, free=("diff_exp", u + 1))
            plan(f"ds{u}b", (2 * u) % 4 + 1, free=("diff_exp", u + 1))
            plan(f"dt{u}", 4 + u % 2, free=("diff_transposed", u + 1))
            if u % 2:
                plan(f"do{u // 2}", 6 + (u // 2) % 2)
        for h in range(4):
            plan(f"rs{h}a", (2 * h) % 4, free=("ret_weights", h + 1))
            plan(f"rs{h}b", (2 * h) % 4 + 1, free=("ret_weights", h + 1))
            plan(f"ro{h}", 6 + h % 2)
        for n in range(4):
            plan(f"mn{n}", n)
        out_loads = {}

        def plan_out(tag, w):
            out_loads[tag] = len(loads)
            for n in range(4):
                last_free = {"wout": ("x_ready", 1), "hout": ("residual", 2), "mout": ("residual", 5)}[tag]
                u = plan(f"{tag}{n}", 4 + n, free=last_free if n == 3 else None)
                load(w[:, :, n * HALF:(n + 1) * HALF], HALF, u.full)

        plan_out("wout", rows(A["w_out"][0]))
        plan("ms_second", 0)
        plan("router", 1, free=("router_sigmoid", 1))
        plan("routeT", 2, free=("route_copied", 1))

        ph = {}
        unit0 = 0

        def plan_units(tag, n, gate, up, down):
            nonlocal unit0
            q = Use()
            q.n, q.unit0, q.L0 = n, unit0, len(loads)
            q.gate, q.up, q.down = gate, up, down
            for e in range(n):
                gb, ub = 2 * (e % 2), 2 * (e % 2) + 1
                x = plan(f"{tag}_up{e}", ub, free=("hidden_ready", unit0 + e + 1))
                plan(f"{tag}_gate{e}", gb, free=x.free)
            for n4 in range(4):
                last_free = {"moe": ("x_ready", 2), "ffn0": ("residual", 1), "ffn1": ("residual", 3),
                             "ffn2": ("residual", 4), "ffn3": ("residual", 6)}[tag]
                plan(f"{tag}_y{n4}", 4 + n4, full=("units_down", unit0 + n), free=last_free if n4 == 3 else None)
            order = [("g", 0), ("u", 0)]
            for e in range(1, n):
                order += [("g", e), ("u", e), ("d", e - 1)]
            order.append(("d", n - 1))
            for kind, e in order:
                if kind == "g":
                    load(("gate", e), HALF, uses[f"{tag}_gate{e}"].full)
                elif kind == "u":
                    load(("up", e), HALF, uses[f"{tag}_up{e}"].full)
                else:
                    load(("down", e), HALF, ("units_down", unit0 + e + 1))
            unit0 += n
            ph[tag] = q

        w1, w3, w2 = A["exp_w1"][0], A["exp_w3"][0], A["exp_w2"][0]
        plan_units("moe", MOE_UNITS, (w1, A["shared_w1"][0]), (w3, A["shared_w3"][0]), (w2, A["shared_w2"][0]))
        plan("mod_first", 0)
        plan("ms_third", 1)
        plan("mod_sum0", 2)

        def plan_ffn(tag, l, s):
            plan_units(tag, FFN_UNITS, A["ffn_w_gate_2"][l, s], A["ffn_w_up_2"][l, s], A["ffn_w_down_2"][l, s])

        def plan_ln(tag):
            plan(f"{tag}_mean", 0)
            plan(f"{tag}_ms", 1)

        plan_ffn("ffn0", 0, 0)
        plan_ln("ln0")
        plan("mod_sum1", 3)
        hyb = rows(A["hyb_w_in_2"][0])
        hyb_slots = [("aq", 0), ("aq", 256), ("ak", 512), ("ak", 768), ("iq", 1536), ("iq", 1792), ("av", 1024),
                     ("av", 1280), ("bq", 2120), ("bq", 2376), ("bq", 2632), ("bq", 2888), ("bq", 3144), ("bq", 3400),
                     ("bz", 3664), ("bz", 3920)]
        L_HYB = len(loads)
        for n, (kind, c0) in enumerate(hyb_slots):
            u = plan(f"hy{n}", n % 4, free=("hy_copied", n + 1) if n < 8 else ("cin_ready", n - 7) if n < 14
                     else ("bz_silu", n - 13))
            load(hyb[:, :, c0:c0 + HALF], HALF, u.full)
        plan("hy_ik", 4, free=("ik_copied", 1))
        plan("hy_iw", 5, free=("iwab_ready", 1))
        for n in range(8):
            plan(f"ix{n}", 6 + n % 2, free=("relu_done", n + 1))

        def plan_attn(tag, heads):
            for h in range(heads):
                plan(f"{tag}_s{h}", h % 2)
                plan(f"{tag}_t{h}", 2 + h % 2, free=("att_transposed", {"dsa": 0, "mla": 8}[tag] + h + 1))
                if h % 2:
                    plan(f"{tag}_o{h // 2}", 4 + (h // 2) % 2)

        plan_attn("dsa", 8)
        for n in range(4):
            plan(f"l2_{n}", n)
        plan("gd_rows", 4, free=("gd_rows_copied", 1))
        plan("gd_cols", 5)
        plan("gd_g0", 6)
        plan("gd_g1", 7, free=("kd_arg", 1))
        plan("gd_b0", 4)
        plan("gd_b1", 5)
        plan("gd_kk0", 0)
        plan("gd_kk1", 1)
        plan("gd_qk0", 2)
        plan("gd_qk1", 3)
        plan("gd_v0", 6)
        plan("gd_v1", 7)
        plan("gd_k0", 4)
        for l in range(7):
            for n in range(2):
                plan(f"gx{l}_{n}", n, free=("inv_x", 2 * l + n + 1))
                if l < 6:
                    plan(f"gd{l}_{n}", 2 + n)
                plan(f"gu{l}_{n}", 4 + n, free=("inv_updated", 2 * l + n + 1))
        plan("gs_vn0", 6, free=("vnew_copied", 1))
        plan("gs_o0", 7)
        plan("gs_s", 0, free=("state_copied", 1))
        plan("gs_r1", 1, free=("rest_ready", 1))
        plan("gs_vn1", 6, free=("vnew_copied", 2))
        plan("gs_o1", 7, free=("delta_out", 1))
        plan("gn0", 2)
        plan("gn1", 3)
        plan_out("hout", rows(A["hyb_w_out_2"][0]))
        plan_ln("ln1")
        plan_ffn("ffn1", 0, 1)
        plan_ln("ln2")
        plan_ffn("ffn2", 1, 0)
        plan_ln("ln3")
        mla = rows(A["mla_w_in_2"][0])
        L_MLA = len(loads)
        for n, (c0, w) in enumerate([(0, 256), (256, 256), (512, 160)]):
            u = plan(f"ml{n}", n, free=("latent_copied", n + 1))
            load(mla[:, :, c0:c0 + w], w, u.full)
        plan("mq_ms", 3)
        plan("mkv_ms", 4)
        plan("mk_rot", 5)
        qup = rows(A["mla_w_q_up_2"][0])
        for n in range(8):
            plan(f"mq{n}", n % 2, free=("mq_raw", n + 1))
            plan(f"mr{n}", 2 + n % 2)
        L_QUP = len(loads)
        for n in range(4):
            load(qup[:, :, n * 384:(n + 1) * 384], 384, uses[f"mq{2 * n + 1}"].full)
        kvup = rows(A["mla_w_kv_up_2"][0])
        for n in range(2):
            for m in range(4):
                plan(f"mk{4 * n + m}", 4 + m % 2, free=("mla_operands", 6 * n + m + 1))
            for m in range(2):
                plan(f"mv{2 * n + m}", 6 + m, free=("mla_operands", 6 * n + 5 + m))
        L_KVUP = len(loads)
        for n in range(2):
            load(kvup[:, :, n * 1024:(n + 1) * 1024], 1024, uses[f"mv{2 * n + 1}"].full)
        plan_attn("mla", 16)
        plan_out("mout", rows(A["mla_w_out_2"][0]))
        plan_ln("ln4")
        plan_ffn("ffn3", 1, 1)
        plan_ln("ln5")
        for n in range(4):
            plan(f"fin{n}", 2 + n, free=("result_ready", n + 1))

        def wait(eng, pair):
            eng.wait_ge(S(pair[0]), pair[1])

        def slot_view(L, width, kt=KT):
            return WR[:, L % SLOTS, 0:kt * width].rearrange("p (k n) -> p k n", k=kt)

        TOK = ar(0, 4, D)
        SQ1 = ar(4096, KT, 512)
        DQ = ar(0, 4, T)
        DK = ar(1024, 4, 2 * T)
        DV = ar(3072, 4, 512)
        RQ = ar(8192, 2, T)
        RK = ar(8704, 2, 2 * T)
        RV = ar(9728, 4, 512)
        RG = ar(11776, 4, T)
        RAW = ar(12800, 2, T)
        RTMP = ar(13312, T)
        PR = ar(13568, 2, 2, 512)
        DIRS = ar(5120, 2, 2, T)
        AT = ar(15616, 2, 4, T)
        EF = ar(6144, 4, T)
        EB = ar(7168, 4, T)
        SD = ar(13568, 2, 4, T)
        MIXED = U_IN
        MSQ = ar(13568, KT, T)
        MRI = ar(15616, KT, T)
        DIST = SQ[:, :, :].rearrange("p (a k) t -> p a k t", a=2)
        ADROW = [buf[0:2, a].rearrange("p b t -> p (b t)") for buf in (SIL, HID) for a in range(2)]
        MACC = ARENA[:, :].rearrange("p (l j n) -> p l j n", l=2, j=MOD_SLOTS)

        AQ, AK, AV, IQ = ar(0, 4, T), ar(1024, 4, T), ar(2048, 2, 512), ar(3072, 4, T)
        IK = ar(4096, T)
        IWAB = ar(4352, 2, 16)
        REL = ar(6720, 2, 2, T)
        SCORE = ar(4912, 2, T)
        WORK = ar(5424, T)
        MAX8 = ar(5680, 8)
        NM = ar(5696, 2, T)
        DISTP = ar(6208, 2, T)
        BIAS = ar(6720, 2, 2, T)
        ATT_T = ar(7744, 2, 2, T)
        CIN = ar(8768, 12, 260)
        LOG = ar(8768, 2, 2, T)
        PRB = ar(9792, 2, 2, T)
        QKV = ar(11888, 12, T)
        BZ = ar(14960, 4, T)
        KCH = ar(15984, 9, P)
        IKW = ar(17136, KT, 144)
        MT, GD, GU, GX = ar(0, 8, P), ar(1024, 8, P), ar(2048, 8, P), ar(3072, 8, P)
        DEC, GA = ar(4096, 8, P), ar(5120, 8, P)
        VB, KTOK = ar(6144, 8, P), ar(7168, 4, P)
        GOFF = ar(7680, 8, P)
        QG, KBG = ar(8768, 8, P), ar(9792, 8, P)
        EGR = ar(10816, 8, P)
        RS_, VN, ST = SQ[:, 0:2, :].rearrange("p a t -> p (a t)"), SQ[:, 2:4, :].rearrange("p a t -> p (a t)"), SQ[:, 4:6, :].rearrange("p a t -> p (a t)")
        OT = ar(17136, 4, T)
        OSQ = ar(7680, 4, T)
        L2SQ, L2R = ar(0, 8, T), ar(2048, 8, T)
        GRW = MEAN[0:4, :]
        GRB = RR[0:4, 0:T]

        CQ, CKV = ar(0, 3, T), ar(768, 2, T)
        CSQ = ar(1280, 5, T)
        QT, KTT = ar(2560, 16, T), ar(6656, 16, T)
        VV = ar(10752, 2, D)
        MLOG, MPRB = ar(12800, 2, 2, T), ar(13824, 2, 2, T)
        MATT = ar(14848, 2, 2, T)
        MNM = ar(15872, 2, T)
        MRAW = ar(16384, 2, 512)
        KROT = ar(17408, 97)
        KRAW = ar(17536, T)
        MTMP = ar(17792, 512)
        MCOS, MSIN = RR[:, 0:T], RR[:, T:2 * T]
        POSF = BC[:, 256:512]

        PROWS = AACC[:, :, :].rearrange("p a n -> p (a n)")[:, 0:512].rearrange("p (a n) -> p a n", a=4)
        route = lambda a: AXS[:, a, 0:128].rearrange("p (t e) -> p t e", t=2)
        ROUTE_S, ROUTE_SEL, ROUTE_X, ROUTE_W = route(0), route(1), route(2), route(3)
        ROUTE_T = AXS[0:N_EXP, 4, :]
        HSEL = GW[:, :, :].rearrange("p a t -> p (a t)").rearrange("p (h n) -> p h n", h=4)
        MRI2 = ar(9792, 4, T)
        POSI = sb("positions", [P, T], I32)
        POSC = sb("position_cols", [P, 2], I32)
        CHKF = sb("chunk_row", [P, T])
        N_PARAM_DMAS = len(PARAMS)
        b_dec = small(0, 8)
        b_rbias = SM[:, 8:72]
        b_alog, b_dt = small(72, 4), small(76, 4)
        s_lam = small(80)
        s_e = small(81, 2)
        s_logg = small(84, 8)
        s_tmp = SM[:, 92:152]
        s_max = small(152, 4)
        s_sum = small(156, 4)
        s_r = small(160, 4)
        s_max2, s_sum2, s_r2 = small(164, 4), small(168, 4), small(172, 4)
        s_gc = small(176, 8)
        s_kd = small(184, 8)
        s_g = small(192, 8)
        s_beta = small(200, 8)
        s_nega = small(208, 4)
        s_posc = small(212, 2)
        s_chc = small(214, 2)
        g1c = small(216, 8)
        sc2 = small(224, 8)
        u_sc, u_sh = small(232, 8), small(240, 8)
        ei_c = small(248, 1)

        def loop_count(tag):
            return 30 if tag == "moe" else (FFN_UNITS - PEELED) // 2

        y_of = lambda kt: PS[:, 4 + kt // 2, (kt % 2) * T:(kt % 2 + 1) * T]
        pi32 = float(np.float32(math.pi))

        block = ctx.enter_context(nc.Block())

        @block.sync
        def _(sp):
            sp.dma_start(K0[:, :], A["k_always"][:, :]).then_inc(S("always_in"), 16)
            for tt in range(2):
                sp.dma_start(TOK[:, tt, :], A["ctx"][0, tt * P:(tt + 1) * P, :]).then_inc(S("tokens_in"), 16)
            for tt in range(2):
                sp.dma_start(TOK[:, 2 + tt, :], A["x"][0, tt * P:(tt + 1) * P, :]).then_inc(S("tokens_in"), 16)

            def fetch(L, view, width, kt=KT):
                if L >= SLOTS:
                    wait(sp, released[L - SLOTS])
                sp.dma_start(slot_view(L, width, kt), view).then_inc(S(f"weights_in{L % SLOTS}"), 16)

            def fetch_all(L0, n, kt=KT):
                for L in range(L0, L0 + n):
                    fetch(L, loads[L][0], loads[L][1], kt)

            fetch_all(L_ADA, 20)
            fetch_all(out_loads["wout"], 4)

            def units(tag):
                q = ph[tag]
                moe = tag == "moe"

                def g_at(e):
                    return q.L0 + (0 if e == 0 else 3 * e - 1)

                def d_at(e):
                    return q.L0 + (3 * e + 4 if e < q.n - 1 else 3 * q.n - 1)

                def src(kind, e):
                    w = {"gate": q.gate, "up": q.up, "down": q.down}[kind]
                    if moe:
                        if isinstance(e, int) and e == N_EXP:
                            w = w[1]
                            return rows(w)
                        w = w[0][bass.ds(e, 1)]
                        return w.rearrange("o (k p) n -> p (o k) n", p=P)
                    if kind == "down":
                        return w[bass.ds(e * HALF, HALF), :].rearrange("(k p) n -> p k n", p=P)
                    return rows(w)[:, :, bass.ds(e * HALF, HALF)]

                def one(e, i=None):
                    eu = e if i is None else e + 2 * i
                    b = e % 2
                    for kind, L in (("gate", g_at(e)), ("up", g_at(e) + 1), ("down", d_at(e - 1) if e else None)):
                        if L is None:
                            continue
                        ev = eu - 1 if kind == "down" else eu
                        if L >= SLOTS:
                            r = released[L - SLOTS]
                            if i is None:
                                wait(sp, r)
                            else:
                                sp.wait_ge(S(r[0]), r[1] + (2 if kind == "down" else 1) * i)
                        dst = slot_view(L, D if kind == "down" else HALF, 2 if kind == "down" else KT)
                        sp.dma_start(dst, src(kind, ev)).then_inc(S(f"weights_in{L % SLOTS}"), 16)
                    if moe and e < N_EXP:
                        if e == 0:
                            sp.wait_ge(S("route_stored"), 16)
                        if e >= 2:
                            sp.wait_ge(S("hidden_ready"), q.unit0 + eu - 1)
                        sp.dma_start(GW[:, b, :], route_rows[bass.ds(eu, 1), :].to_broadcast([P, T])).then_inc(
                            S(f"route_in{b}"), 16)

                for e in range(PEELED):
                    one(e)
                with sp.Fori(0, loop_count(tag)) as i:
                    one(PEELED, i)
                    one(PEELED + 1, i)
                for e in range(PEELED + 2 * loop_count(tag), q.n):
                    one(e)
                L = q.L0 + 3 * q.n - 1
                wait(sp, released[L - SLOTS])
                sp.dma_start(slot_view(L, D, 2), src("down", q.n - 1)).then_inc(S(f"weights_in{L % SLOTS}"), 16)

            units("moe")
            units("ffn0")
            fetch_all(L_HYB, 16)
            fetch_all(out_loads["hout"], 4)
            units("ffn1")
            units("ffn2")
            fetch_all(L_MLA, 3)
            fetch_all(L_QUP, 4, 3)
            fetch_all(L_KVUP, 2, 2)
            fetch_all(out_loads["mout"], 4)
            units("ffn3")
            for tt in range(TT):
                sp.wait_ge(S("result_ready"), 2 * tt + 2)
                sp.dma_start(out[0, tt * P:(tt + 1) * P, :], ar(0, 2, D)[:, tt, :]).then_inc(S("out_stored"), 16)
            sp.wait_ge(S("out_stored"), 16 * TT)

        @block.tensor
        def _(pe):
            mm = nc.tensor.matmul

            def weights(L):
                pe.wait_ge(S(f"weights_in{L % SLOTS}"), 16 * (L // SLOTS + 1))

            def open_bank(name):
                u = uses[name]
                if u.prev is not None:
                    wait(pe, u.prev.free)
                return PS[:, u.bank]

            def full(ins, name):
                ins.then_inc(S(uses[name].full[0]), 1)

            pe.wait_ge(S("always_in"), 16)
            pe.wait_ge(S("tokens_in"), 64)
            for n in range(8):
                tt, half = n // 2, n % 2
                b = open_bank(f"xt{n}")
                for q in range(4):
                    kt = 4 * half + q
                    last = nc.tensor.transpose(b[:, q * P:(q + 1) * P], TOK[:, tt, kt * P:(kt + 1) * P], IDN)
                full(last, f"xt{n}")
            pe.wait_ge(S("params_in"), 16 * N_PARAM_DMAS)
            b = open_bank("params")
            for n, (lo, hi) in enumerate(PARAM_TILES):
                last = nc.tensor.transpose(b[:, lo:hi], PROWS[0:hi - lo, n, :], IDN[0:hi - lo, 0:hi - lo])
            full(last, "params")
            pe.wait_ge(S("squared"), 2)
            b = open_bank("ms_first")
            for kt in range(KT):
                last = mm(b[:, :], ONES, SQ1[:, kt, :], start=kt == 0, stop=kt == KT - 1)
            full(last, "ms_first")
            pe.wait_ge(S("silu_c"), 1)
            for n in range(8):
                L = L_ADA + n
                if n % 2 == 0:
                    b = open_bank(f"ada_row{n // 2}")
                weights(L)
                w = slot_view(L, HALF)
                for kt in range(KT):
                    last = mm(b[0:2, (n % 2) * HALF:(n % 2 + 1) * HALF], CS[:, 0:2, kt], w[:, kt, :],
                              start=kt == 0, stop=kt == KT - 1)
                last.then_inc(S("ada_slot_done"), 1)
            b = open_bank("ada_col")
            for q in range(16):
                if q % 4 == 0:
                    pe.wait_ge(S("ada_row_copied"), q // 4 + 1)
                last = nc.tensor.transpose(b[:, 2 * q:2 * q + 2], ADROW[q // 4][:, (q % 4) * P:(q % 4 + 1) * P],
                                           IDN[0:2, 0:2])
            full(last, "ada_col")

            pe.wait_ge(S("h_ready"), 1)

            def swap(j):
                b = open_bank(f"sw{j}")
                pe.wait_ge(S("raw_ready"), j + 1)
                full(mm(b[:, 0:T], SWP, RAW[:, j % 2], start=True, stop=True), f"sw{j}")

            late = open_bank("ada_late")

            def ada_late(a):
                pe.wait_ge(S("ada_acc"), a + 1)
                for half in range(2):
                    last = mm(late[:, 2 * a + half:2 * a + half + 1], AACC[:, a % 4, half * P:(half + 1) * P],
                              ONES[:, 0:1], start=True, stop=True)
                last.then_inc(S("ada_acc_used"), 1)

            for j in range(12):
                L = L_PROJ + j // 2
                if j % 2 == 0:
                    weights(L)
                w = slot_view(L, HALF)[:, :, (j % 2) * P:(j % 2 + 1) * P]
                wide = not (j < 4 or j in (8, 9))
                b = open_bank(f"pj{j}")
                rhs = H[:, :, :] if wide else H[:, :, T:2 * T]
                for kt in range(KT):
                    last = mm(b[:, 0:(2 * T if wide else T)], w[:, kt, :], rhs[:, kt, :], start=kt == 0, stop=kt == KT - 1)
                full(last, f"pj{j}")
                if j:
                    swap(j - 1)
                if j >= 8:
                    ada_late(j - 8)
            swap(11)
            for n in range(8):
                L = L_PROJ + 6 + n // 2
                weights(L)
                w = slot_view(L, HALF)
                b = open_bank(f"vt{n}")
                for m in range(2):
                    tt = 2 * (n % 2) + m
                    for kt in range(KT):
                        last = mm(b[:, m * HALF:(m + 1) * HALF], H[:, kt, tt * P:(tt + 1) * P], w[:, kt, :],
                                  start=kt == 0, stop=kt == KT - 1)
                full(last, f"vt{n}")
                ada_late(4 + n)
            for n in range(2):
                L = L_PROJ + 10 + n
                weights(L)
                w = slot_view(L, HALF)
                b = open_bank(f"rg{n}")
                for m in range(2):
                    for kt in range(KT):
                        last = mm(b[:, m * T:(m + 1) * T], w[:, kt, m * P:(m + 1) * P], H[:, kt, T:2 * T],
                                  start=kt == 0, stop=kt == KT - 1)
                full(last, f"rg{n}")
                ada_late(12 + 2 * n)
                if n == 0:
                    ada_late(13)
            pe.wait_ge(S("ada_acc"), 16)
            for half in range(2):
                last = mm(late[:, 30 + half:31 + half], AACC[:, 15 % 4, half * P:(half + 1) * P], ONES[:, 0:1],
                          start=True, stop=True)
            full(last, "ada_late")

            pe.wait_ge(S("roped"), 12)
            pe.wait_ge(S("values_copied"), 8)

            def diff_scores(u):
                h, qt = u // 2, u % 2
                open_bank(f"ds{u}a")
                open_bank(f"ds{u}b")
                for m in range(2):
                    b = PS[:, uses[f"ds{u}a"].bank + m]
                    full(mm(b[:, :], DQ[64 * m:64 * m + 64, h, qt * P:(qt + 1) * P], DK[64 * m:64 * m + 64, h, :],
                            start=True, stop=True), f"ds{u}" + "ab"[m])

            def diff_product(h):
                pe.wait_ge(S("diff_transposed"), 2 * h + 2)
                b = open_bank(f"do{h}")
                for kb in range(4):
                    last = mm(b[:, 0:T], DV[:, kb, h * P:(h + 1) * P], AT[:, h % 2, kb, :], start=kb == 0, stop=kb == 3)
                full(last, f"do{h}")

            diff_scores(0)
            for u in range(8):
                if u < 7:
                    diff_scores(u + 1)
                pe.wait_ge(S("diff_weights"), u + 1)
                b = open_bank(f"dt{u}")
                for kb in range(4):
                    last = nc.tensor.transpose(b[:, kb * P:(kb + 1) * P], PR[:, u % 2, 0, kb * P:(kb + 1) * P], IDN)
                full(last, f"dt{u}")
                if u >= 2 and u % 2 == 0:
                    diff_product(u // 2 - 1)
            diff_product(3)

            def ret_scores(h):
                open_bank(f"rs{h}a")
                open_bank(f"rs{h}b")
                r = slice(64 * (h % 2), 64 * (h % 2) + 64)
                for m in range(2):
                    b = PS[:, uses[f"rs{h}a"].bank + m]
                    for q in range(2):
                        kb = 2 * m + q
                        last = mm(b[:, q * T:(q + 1) * T], RK[r, h // 2, kb * P:(kb + 1) * P], RQ[r, h // 2, :],
                                  start=True, stop=True)
                    full(last, f"rs{h}" + "ab"[m])

            ret_scores(0)
            for h in range(4):
                if h < 3:
                    ret_scores(h + 1)
                pe.wait_ge(S("ret_weights"), h + 1)
                b = open_bank(f"ro{h}")
                for kb in range(4):
                    last = mm(b[:, 0:T], RV[:, kb, h * P:(h + 1) * P], SD[:, h % 2, kb, :], start=kb == 0, stop=kb == 3)
                full(last, f"ro{h}")
            pe.wait_ge(S("heads_squared"), 1)
            for n in range(4):
                b = open_bank(f"mn{n}")
                full(mm(b[:, :], ONES, MSQ[:, 2 * n:2 * n + 2, :], start=True, stop=True), f"mn{n}")

            def project_out(tag, k):
                pe.wait_ge(S("mix_ready"), k)
                for n in range(4):
                    L = out_loads[tag] + n
                    weights(L)
                    w = slot_view(L, HALF)
                    b = open_bank(f"{tag}{n}")
                    for m in range(2):
                        for kt in range(KT):
                            last = mm(b[:, m * T:(m + 1) * T], w[:, kt, m * P:(m + 1) * P], MIX[:, kt, :],
                                      start=kt == 0, stop=kt == KT - 1)
                    full(last, f"{tag}{n}")

            project_out("wout", 1)

            def feature_sum(name, src, ready, k):
                pe.wait_ge(S(ready), k)
                b = open_bank(name)
                for kt in range(KT):
                    last = mm(b[:, 0:T], ONES, src[:, kt, :], start=kt == 0, stop=kt == KT - 1)
                full(last, name)

            feature_sum("ms_second", SQ, "squared", 3)
            pe.wait_ge(S("h_ready"), 2)
            pe.wait_ge(S("router_in"), 16)
            b = open_bank("router")
            for tt in range(TT):
                for kt in range(KT):
                    last = mm(b[:, tt * N_EXP:(tt + 1) * N_EXP], U_IN[:, kt, tt * P:(tt + 1) * P], RW[:, kt, :],
                              start=kt == 0, stop=kt == KT - 1)
            full(last, "router")

            def units(tag, between=None):
                q = ph[tag]
                g_at = lambda e: q.L0 + (0 if e == 0 else 3 * e - 1)
                d_at = lambda e: q.L0 + (3 * e + 4 if e < q.n - 1 else 3 * q.n - 1)

                def up(eng_e, i=None):
                    e = eng_e
                    x = uses[f"{tag}_up{e}"]
                    gb = uses[f"{tag}_gate{e}"]
                    n = 0 if i is None else i
                    if gb.prev is not None and i is None:
                        wait(pe, gb.prev.free)
                    if x.prev is not None:
                        pe.wait_ge(S(x.prev.free[0]), x.prev.free[1] + 2 * n)
                    for L, bank, u in ((g_at(e), gb.bank, gb), (g_at(e) + 1, x.bank, x)):
                        pe.wait_ge(S(f"weights_in{L % SLOTS}"), 16 * (L // SLOTS + 1 + n))
                        w = slot_view(L, HALF)
                        for m in range(2):
                            for kt in range(KT):
                                last = mm(PS[:, bank, m * T:(m + 1) * T], w[:, kt, m * P:(m + 1) * P], U_IN[:, kt, :],
                                          start=kt == 0, stop=kt == KT - 1)
                        last.then_inc(S(u.full[0]), 1)

                def down(e, i=None, first=False, last_unit=False):
                    n = 0 if i is None else i
                    L = d_at(e)
                    pe.wait_ge(S("hidden_ready"), q.unit0 + e + 1 + 2 * n)
                    pe.wait_ge(S(f"weights_in{L % SLOTS}"), 16 * (L // SLOTS + 1 + n))
                    w = slot_view(L, D, 2)
                    for kt in range(KT):
                        for m in range(2):
                            ins = mm(y_of(kt), w[:, m, kt * P:(kt + 1) * P], HID[:, e % 2, m, :],
                                     start=first and m == 0 and kt % 2 == 0, stop=last_unit and m == 1 and kt % 2 == 1)
                    ins.then_inc(S("units_down"), 1)

                for e in range(PEELED):
                    up(e)
                    if e == 1:
                        for n4 in range(4):
                            open_bank(f"{tag}_y{n4}")
                    if e:
                        down(e - 1, first=e == 1)
                with pe.Fori(0, loop_count(tag)) as i:
                    for e in (PEELED, PEELED + 1):
                        up(e, i)
                        down(e - 1, i)
                for e in range(PEELED + 2 * loop_count(tag), q.n):
                    up(e)
                    down(e - 1)
                down(q.n - 1, last_unit=True)

            pe.wait_ge(S("route_weights"), 1)
            b = open_bank("routeT")
            for tt in range(TT):
                last = nc.tensor.transpose(b[0:N_EXP, tt * P:(tt + 1) * P], ROUTE_W[:, tt, :], IDN)
            full(last, "routeT")

            units("moe")
            pe.wait_ge(S("mod_acc"), 2 * MOD_SLOTS)

            def mod_sums(name, l, lo, hi):
                b = open_bank(name)
                for j in range(lo, hi):
                    last = mm(b[:, j:j + 1], MACC[:, l, j // 2, (j % 2) * P:(j % 2 + 1) * P], ONES[:, 0:1],
                              start=True, stop=True)
                full(last, name)

            mod_sums("mod_first", 0, 0, 24)
            feature_sum("ms_third", SQ, "squared", 4)
            mod_sums("mod_sum0", 0, 24, 72)

            def layer_norm(tag, k, ytag):
                b = open_bank(f"{tag}_mean")
                for kt in range(KT):
                    if kt % 2 == 0:
                        wait(pe, uses[f"{ytag}{kt // 2}"].free)
                    last = mm(b[:, 0:T], ONES, XS[:, 0, kt, :], start=kt == 0, stop=kt == KT - 1)
                full(last, f"{tag}_mean")
                b = open_bank(f"{tag}_ms")
                for kt in range(KT):
                    if kt % 4 == 0:
                        pe.wait_ge(S("squared_half"), 2 * k - 1 + kt // 4)
                    last = mm(b[:, 0:T], ONES, SQ[:, kt, :], start=kt == 0, stop=kt == KT - 1)
                full(last, f"{tag}_ms")

            pe.wait_ge(S("h_ready"), 3)
            units("ffn0")
            layer_norm("ln0", 1, "ffn0_y")
            mod_sums("mod_sum1", 1, 0, 72)

            def indexer():
                pe.wait_ge(S("ikw_in"), 48)
                b = open_bank("hy_ik")
                for kt in range(KT):
                    last = mm(b[:, 0:T], IKW[:, kt, 0:128], U_IN[:, kt, :], start=kt == 0, stop=kt == KT - 1)
                full(last, "hy_ik")
                b = open_bank("hy_iw")
                for tt in range(TT):
                    for kt in range(KT):
                        last = mm(b[:, tt * 16:(tt + 1) * 16], U_IN[:, kt, tt * P:(tt + 1) * P], IKW[:, kt, 128:144],
                                  start=kt == 0, stop=kt == KT - 1)
                full(last, "hy_iw")
                pe.wait_ge(S("hy_copied"), 6)
                pe.wait_ge(S("ik_copied"), 1)
                for n in range(8):
                    r = slice(64 * (n % 2), 64 * (n % 2) + 64)
                    b = open_bank(f"ix{n}")
                    for qt in range(TT):
                        last = mm(b[:, qt * T:(qt + 1) * T], IQ[r, n // 2, qt * P:(qt + 1) * P], IK[r, :],
                                  start=True, stop=True)
                    full(last, f"ix{n}")

            pe.wait_ge(S("h_ready"), 4)
            for n, (kind, c0) in enumerate(hyb_slots):
                if n == 6:
                    indexer()
                L = L_HYB + n
                weights(L)
                w = slot_view(L, HALF)
                b = open_bank(f"hy{n}")
                for m in range(2):
                    for kt in range(KT):
                        if kind == "av":
                            last = mm(b[:, m * T:(m + 1) * T], U_IN[:, kt, m * P:(m + 1) * P], w[:, kt, :],
                                      start=kt == 0, stop=kt == KT - 1)
                        else:
                            last = mm(b[:, m * T:(m + 1) * T], w[:, kt, m * P:(m + 1) * P], U_IN[:, kt, :],
                                      start=kt == 0, stop=kt == KT - 1)
                full(last, f"hy{n}")
            pe.wait_ge(S("hy_copied"), 8)

            def attention(tag, heads, score, value, probs, att):
                k0 = {"dsa": 0, "mla": 8}[tag]

                def scores(h):
                    b = open_bank(f"{tag}_s{h}")
                    for qt in range(TT):
                        q_ap, k_ap = score(h, qt)
                        last = mm(b[:, qt * T:(qt + 1) * T], q_ap, k_ap, start=True, stop=True)
                    full(last, f"{tag}_s{h}")

                def product(h):
                    pe.wait_ge(S("att_transposed"), k0 + h + 1)
                    if h % 2 == 0:
                        open_bank(f"{tag}_o{h // 2}")
                    o = PS[:, uses[f"{tag}_o{h // 2}"].bank]
                    for kb in range(TT):
                        last = mm(o[:, (h % 2) * T:(h % 2 + 1) * T], value(h // 2, kb), att[:, h % 2, kb, :],
                                  start=kb == 0, stop=kb == TT - 1)
                    if h % 2 == 0:
                        last.then_inc(S("att_even"), 1)
                    else:
                        full(last, f"{tag}_o{h // 2}")

                scores(0)
                for h in range(heads):
                    if h < heads - 1:
                        scores(h + 1)
                    pe.wait_ge(S("att_weights"), k0 + h + 1)
                    b = open_bank(f"{tag}_t{h}")
                    for kb in range(TT):
                        for qt in range(TT):
                            last = nc.tensor.transpose(b[:, kb * T + qt * P:kb * T + (qt + 1) * P],
                                                       probs[:, h % 2, qt, kb * P:(kb + 1) * P], IDN)
                    full(last, f"{tag}_t{h}")
                    if h:
                        product(h - 1)
                product(heads - 1)

            attention("dsa", 8,
                      lambda h, qt: (AQ[64 * (h % 2):64 * (h % 2) + 64, h // 2, qt * P:(qt + 1) * P],
                                     AK[64 * (h % 2):64 * (h % 2) + 64, h // 2, :]),
                      lambda pair, kb: AV[:, kb, pair * P:(pair + 1) * P], PRB, ATT_T)

            pe.wait_ge(S("qk_squared"), 1)
            for n in range(4):
                b = open_bank(f"l2_{n}")
                full(mm(b[:, :], ONES, L2SQ[:, 2 * n:2 * n + 2, :], start=True, stop=True), f"l2_{n}")
            pe.wait_ge(S("gates"), 1)
            pe.wait_ge(S("chunk_in"), 16)
            pe.wait_ge(S("heads_in"), 16)
            incl_, strict_ = KCH[:, 7, :], KCH[:, 8, :]
            b = open_bank("gd_rows")
            for tt in range(TT):
                mm(b[0:4, tt * P:(tt + 1) * P], s_g[:, 4 * tt:4 * tt + 4], incl_, start=True, stop=True)
            for tt in range(TT):
                last = nc.tensor.transpose(b[0:4, T + tt * P:T + (tt + 1) * P], s_beta[:, 4 * tt:4 * tt + 4], IDN)
            full(last, "gd_rows")
            pe.wait_ge(S("gd_rows_copied"), 1)
            b = open_bank("gd_cols")
            for tt in range(TT):
                last = nc.tensor.transpose(b[:, 4 * tt:4 * tt + 4], GRW[:, tt * P:(tt + 1) * P], IDN[0:4, 0:4])
            full(last, "gd_cols")
            for nm, row in (("g", GRW), ("b", GRB)):
                for n in range(2):
                    b = open_bank(f"gd_{nm}{n}")
                    for m in range(2):
                        h = 2 * n + m
                        last = mm(b[:, m * T:(m + 1) * T], HSEL[0:4, h, :], row, start=True, stop=True)
                    full(last, f"gd_{nm}{n}")
            pe.wait_ge(S("qk_normed"), 1)
            for nm, a, c in (("kk", 4, 4), ("qk", 4, 0)):
                for n in range(2):
                    b = open_bank(f"gd_{nm}{n}")
                    for m in range(4):
                        h, tt = 2 * n + m // 2, m % 2
                        ts_ = slice(tt * P, (tt + 1) * P)
                        last = mm(b[:, m * P:(m + 1) * P], QKV[:, a + h, ts_], QKV[:, c + h, ts_], start=True, stop=True)
                    full(last, f"gd_{nm}{n}")
            for n in range(2):
                b = open_bank(f"gd_v{n}")
                for m in range(4):
                    h, tt = 2 * n + m // 2, m % 2
                    last = nc.tensor.transpose(b[:, m * P:(m + 1) * P], QKV[:, 8 + h, tt * P:(tt + 1) * P], IDN)
                full(last, f"gd_v{n}")
            b = open_bank("gd_k0")
            for h in range(4):
                last = nc.tensor.transpose(b[:, h * P:(h + 1) * P], QKV[:, 4 + h, 0:P], IDN)
            full(last, "gd_k0")
            for l in range(7):
                for n in range(2):
                    pe.wait_ge(S("inv_masked"), 2 * l + n + 1)
                    if l:
                        pe.wait_ge(S("inv_updated"), 2 * l + n - 1)
                    b = open_bank(f"gx{l}_{n}")
                    for m in range(4):
                        pr = 4 * n + m
                        last = mm(b[:, m * P:(m + 1) * P], GOFF[:, pr, :], GD[:, pr, :], start=True, stop=True)
                    full(last, f"gx{l}_{n}")
                for n in range(2):
                    pe.wait_ge(S("inv_x"), 2 * l + n + 1)
                    if l < 6:
                        b = open_bank(f"gd{l}_{n}")
                        for m in range(4):
                            pr = 4 * n + m
                            last = mm(b[:, m * P:(m + 1) * P], GU[:, pr, :], GX[:, pr, :], start=True, stop=True)
                        full(last, f"gd{l}_{n}")
                    b = open_bank(f"gu{l}_{n}")
                    for m in range(4):
                        pr = 4 * n + m
                        last = mm(b[:, m * P:(m + 1) * P], GX[:, pr, :], GU[:, pr, :], start=True, stop=True)
                    full(last, f"gu{l}_{n}")
            pe.wait_ge(S("inv_updated"), 14)
            pe.wait_ge(S("gd_operands"), 1)
            VBv, RSv = VB, RS_.rearrange("p (h e) -> p h e", h=4)
            VNv, STv = VN.rearrange("p (h e) -> p h e", h=4), ST.rearrange("p (h e) -> p h e", h=4)
            b = open_bank("gs_vn0")
            for h in range(4):
                last = mm(b[:, h * P:(h + 1) * P], GU[:, 2 * h, :], VBv[:, 2 * h, :], start=True, stop=True)
            full(last, "gs_vn0")
            pe.wait_ge(S("vnew_copied"), 1)
            b = open_bank("gs_s")
            for h in range(4):
                last = mm(b[:, h * P:(h + 1) * P], KTOK[:, h, :], VNv[:, h, :], start=True, stop=True)
            full(last, "gs_s")
            b = open_bank("gs_o0")
            for h in range(4):
                last = mm(b[:, h * P:(h + 1) * P], VNv[:, h, :], GA[:, 2 * h, :], start=True, stop=True)
            full(last, "gs_o0")
            pe.wait_ge(S("state_copied"), 1)
            b = open_bank("gs_r1")
            for h in range(4):
                last = mm(b[:, h * P:(h + 1) * P], KBG[:, 2 * h + 1, :], STv[:, h, :], start=True, stop=True)
            full(last, "gs_r1")
            pe.wait_ge(S("rest_ready"), 1)
            b = open_bank("gs_vn1")
            for h in range(4):
                last = mm(b[:, h * P:(h + 1) * P], GU[:, 2 * h + 1, :], RSv[:, h, :], start=True, stop=True)
            full(last, "gs_vn1")
            pe.wait_ge(S("vnew_copied"), 2)
            b = open_bank("gs_o1")
            for h in range(4):
                mm(b[:, h * P:(h + 1) * P], VNv[:, h, :], GA[:, 2 * h + 1, :], start=True, stop=False)
                last = mm(b[:, h * P:(h + 1) * P], STv[:, h, :], QG[:, 2 * h + 1, :], start=False, stop=True)
            full(last, "gs_o1")
            pe.wait_ge(S("delta_squared"), 1)
            for n in range(2):
                b = open_bank(f"gn{n}")
                full(mm(b[:, :], ONES, OSQ[:, 2 * n:2 * n + 2, :], start=True, stop=True), f"gn{n}")
            project_out("hout", 2)
            layer_norm("ln1", 2, "hout")
            pe.wait_ge(S("h_ready"), 5)
            units("ffn1")
            layer_norm("ln2", 3, "ffn1_y")
            pe.wait_ge(S("h_ready"), 6)
            units("ffn2")
            layer_norm("ln3", 4, "ffn2_y")

            pe.wait_ge(S("h_ready"), 7)
            for n in range(2):
                L = L_MLA + n
                weights(L)
                w = slot_view(L, HALF)
                b = open_bank(f"ml{n}")
                for m in range(2):
                    for kt in range(KT):
                        last = mm(b[:, m * T:(m + 1) * T], w[:, kt, m * P:(m + 1) * P], U_IN[:, kt, :],
                                  start=kt == 0, stop=kt == KT - 1)
                full(last, f"ml{n}")
            L = L_MLA + 2
            weights(L)
            w = slot_view(L, 160)
            b = open_bank("ml2")
            for kt in range(KT):
                mm(b[:, 0:T], w[:, kt, 0:P], U_IN[:, kt, :], start=kt == 0, stop=kt == KT - 1)
            for kt in range(KT):
                last = mm(b[0:C_QK, T:2 * T], w[:, kt, 64:160], U_IN[:, kt, :], start=kt == 0, stop=kt == KT - 1)
            full(last, "ml2")
            pe.wait_ge(S("latent_squared"), 1)
            b = open_bank("mq_ms")
            for kt in range(3):
                last = mm(b[:, 0:T], ONES, CSQ[:, kt, :], start=kt == 0, stop=kt == 2)
            full(last, "mq_ms")
            b = open_bank("mkv_ms")
            for kt in range(2):
                last = mm(b[:, 0:T], ONES, CSQ[:, 3 + kt, :], start=kt == 0, stop=kt == 1)
            full(last, "mkv_ms")
            pe.wait_ge(S("rot_in"), 16)
            b = open_bank("mk_rot")
            full(mm(b[0:C_QK, 0:T], KROT[0:C_QK, 0:C_QK], KRAW[0:C_QK, :], start=True, stop=True), "mk_rot")
            pe.wait_ge(S("latent_normed"), 1)

            def rotate_q(n):
                pe.wait_ge(S("mq_raw"), n + 1)
                b = open_bank(f"mr{n}")
                full(mm(b[0:C_QK, :], KROT[0:C_QK, 0:C_QK], MRAW[0:C_QK, n % 2, :], start=True, stop=True), f"mr{n}")

            for n in range(8):
                L = L_QUP + n // 2
                weights(L)
                w = slot_view(L, 384, 3)
                b = open_bank(f"mq{n}")
                for m in range(2):
                    c0 = C_QK * (2 * (n % 2) + m)
                    for kt in range(3):
                        last = mm(b[0:C_QK, m * T:(m + 1) * T], w[:, kt, c0:c0 + C_QK], CQ[:, kt, :],
                                  start=kt == 0, stop=kt == 2)
                full(last, f"mq{n}")
                if n:
                    rotate_q(n - 1)
            rotate_q(7)
            for n in range(2):
                L = L_KVUP + n
                weights(L)
                w = slot_view(L, 1024, 2)
                for m in range(4):
                    b = open_bank(f"mk{4 * n + m}")
                    for a in range(2):
                        c0 = P * (2 * m + a)
                        for kt in range(2):
                            last = mm(b[0:DH, a * T:(a + 1) * T], w[:, kt, c0:c0 + DH], CKV[:, kt, :],
                                      start=kt == 0, stop=kt == 1)
                    full(last, f"mk{4 * n + m}")
                for tt in range(TT):
                    b = open_bank(f"mv{2 * n + tt}")
                    for kt in range(2):
                        wv = w[:, kt, :].rearrange("p (h c) -> p h c", h=8)[:, :, DH:2 * DH]
                        last = mm(b[:, :].rearrange("p (h c) -> p h c", h=8), CKV[:, kt, tt * P:(tt + 1) * P], wv,
                                  start=kt == 0, stop=kt == 1)
                    full(last, f"mv{2 * n + tt}")
            pe.wait_ge(S("mla_operands"), 12)
            pe.wait_ge(S("q_rotated"), 8)
            pe.wait_ge(S("k_rotated"), 1)
            attention("mla", 16,
                      lambda h, qt: (QT[0:C_QK, h, qt * P:(qt + 1) * P], KTT[0:C_QK, h, :]),
                      lambda pair, kb: VV[:, kb, pair * P:(pair + 1) * P], MPRB, MATT)
            project_out("mout", 3)
            layer_norm("ln4", 5, "mout")
            pe.wait_ge(S("h_ready"), 8)
            units("ffn3")
            layer_norm("ln5", 6, "ffn3_y")
            pe.wait_ge(S("result_features"), 1)
            for n in range(4):
                tt, half = n // 2, n % 2
                b = open_bank(f"fin{n}")
                for q in range(4):
                    kt = 4 * half + q
                    last = nc.tensor.transpose(b[:, q * P:(q + 1) * P], X[:, kt, tt * P:(tt + 1) * P], IDN)
                full(last, f"fin{n}")

        ROOT = {n: k + 1 for k, n in enumerate(["first", "heads", "second", "third", "ln0", "l2", "delta", "ln1", "ln2",
                                                "ln3", "latent", "ln4", "ln5"])}
        even_k0 = {"dsa": 0, "mla": 4}
        att_k0 = {"dsa": 0, "mla": 8}

        @block.scalar
        def _(act):
            go = nc.scalar.activation

            def own(name, n):
                act.wait_ge(S(name), n)

            def full(name):
                wait(act, uses[name].full)
                return PS[:, uses[name].bank]

            def freed(ins, name):
                ins.then_inc(S(uses[name].free[0]), 1)

            for nm, (c0, n) in PARAMS.items():
                t_ = [k for k, (lo, hi) in enumerate(PARAM_TILES) if lo <= c0 < hi][0]
                r0 = c0 - PARAM_TILES[t_][0]
                act.dma_start(PROWS[r0:r0 + n, t_, :], A["rows_" + nm]).then_inc(S("params_in"), 16)
            act.dma_start(SQ[:, :, :].rearrange("p a t -> p (a t)"), A["k_dist"][:, :]).then_inc(S("dist_in"), 16)
            act.dma_start(RW[:, :, :], rows(A["router_w"][0])).then_inc(S("router_in"), 16)

            for n in (1, 3, 5, 7):
                b = full(f"xt{n}")
                tt, half = n // 2, n % 2
                dst = XS[:, tt // 2, 4 * half:4 * half + 4, (tt % 2) * P:(tt % 2 + 1) * P]
                freed(go(dst, b.rearrange("p (k n) -> p k n", k=4), ACT.Copy), f"xt{n}")
            act.wait_ge(S("cols_ready"), 1)
            c0 = PARAMS["c"][0]
            go(CS[:, :, :], COLS[:, c0:c0 + 24].rearrange("p (j k) -> p j k", j=3), ACT.Silu).then_inc(S("silu_c"), 1)
            act.wait_ge(S("xt_by_vector"), 4)
            own("xt_by_scalar", 4)
            for s in range(2):
                go(SQ1[:, :, s * T:(s + 1) * T], XS[:, s], ACT.Square).then_inc(S("squared"), 1)

            def root(name, ap):
                act.wait_ge(S("recip"), ROOT[name])
                go(ap, ap, ACT.Sqrt).then_inc(S("rinv"), 1)

            root("first", RR[:, :])
            for n in range(4):
                b = full(f"ada_row{n}")
                freed(go(ADROW[n], b[0:2, :], ACT.Copy), f"ada_row{n}")
            act.wait_ge(S("softplus_abs"), 1)
            go(s_tmp[:, 8:16], s_tmp[:, 0:8], ACT.Exp, scale=-1.0).then_inc(S("softplus_exp"), 1)
            act.wait_ge(S("lam_sums"), 1)
            go(s_e, s_e, ACT.Exp).then_inc(S("lam_exp"), 1)
            ctx_copies = 0
            for j in range(12):
                b = full(f"pj{j}")
                wide = not (j < 4 or j in (8, 9))
                if wide:
                    dst = DK[:, j - 4, 0:T] if j < 8 else RK[:, j - 10, 0:T]
                    go(dst, b[:, 0:T], ACT.Copy)
                if j >= 2:
                    act.wait_ge(S("roped"), j - 1)
                src = b[:, T:2 * T] if wide else b[:, 0:T]
                freed(go(RAW[:, j % 2], src, ACT.Copy), f"pj{j}")
            for n in range(8):
                b = full(f"vt{n}")
                dst = (DV if n < 4 else RV)[:, 2 * (n % 2):2 * (n % 2) + 2, ((n // 2) % 2) * HALF:((n // 2) % 2 + 1) * HALF]
                freed(go(dst, b.rearrange("p (a n) -> p a n", a=2), ACT.Copy), f"vt{n}")
            for n in range(2):
                b = full(f"rg{n}")
                freed(go(RG[:, 2 * n:2 * n + 2, :], b.rearrange("p (a n) -> p a n", a=2), ACT.Silu), f"rg{n}")

            def diff_exp(u):
                act.wait_ge(S("diff_max"), u + 1)
                if u >= 2:
                    wait(act, uses[f"dt{u - 2}"].full)
                for m in range(2):
                    b = full(f"ds{u}" + "ab"[m])
                    k = 2 * (u % 2) + m
                    ins = go(PR[:, u % 2, m, :], b, ACT.Exp, bias=s_max[:, k:k + 1], scale=0.125,
                             accum_out=s_sum[:, k:k + 1])
                freed(ins, f"ds{u}a")

            diff_exp(0)
            for u in range(8):
                if u < 7:
                    diff_exp(u + 1)
                b = full(f"dt{u}")
                h, qt = u // 2, u % 2
                if h >= 2:
                    wait(act, uses[f"do{h - 2}"].full)
                freed(go(AT[:, h % 2, :, qt * P:(qt + 1) * P], b.rearrange("p (k n) -> p k n", k=4), ACT.Copy), f"dt{u}")
            act.wait_ge(S("dist_in"), 16)
            act.wait_ge(S("logg"), 1)
            act.wait_ge(S("h_ready"), 1)
            for h in range(4):
                if h:
                    act.wait_ge(S("ret_weights"), h)
                go(EF, DIST[:, 0], ACT.Exp, scale=s_logg[:, h:h + 1])
                go(EB, DIST[:, 1], ACT.Exp, scale=s_logg[:, 4 + h:5 + h]).then_inc(S("decay_exp"), 1)
            act.wait_ge(S("mixed"), 1)
            go(MSQ, MIXED, ACT.Square).then_inc(S("heads_squared"), 1)
            root("heads", MRI)
            act.wait_ge(S("x_ready"), 1)
            go(SQ[:, :, :], X, ACT.Square).then_inc(S("squared"), 1)
            root("second", RR[:, 0:T])
            b = full("router")
            freed(go(ROUTE_S, b[:, 0:128].rearrange("p (t e) -> p t e", t=2), ACT.Sigmoid), "router")
            b = full("routeT")
            freed(go(ROUTE_T, b[0:N_EXP, 0:T], ACT.Copy), "routeT")
            own("route_copied", 1)
            act.dma_start(route_rows[:, :], ROUTE_T).then_inc(S("route_stored"), 16)

            def units(tag):
                q = ph[tag]

                def one(e, i=None):
                    n = 0 if i is None else i
                    g = uses[f"{tag}_gate{e}"]
                    act.wait_ge(S(g.full[0]), g.full[1] + n)
                    if q.unit0 + e >= 2:
                        act.wait_ge(S("hidden_ready"), q.unit0 + e - 1 + 2 * n)
                    go(SIL[:, e % 2].rearrange("p a t -> p (a t)"), PS[:, g.bank], ACT.Silu).then_inc(S("silu_gate"), 1)

                for e in range(PEELED):
                    one(e)
                with act.Fori(0, loop_count(tag)) as i:
                    one(PEELED, i)
                    one(PEELED + 1, i)
                for e in range(PEELED + 2 * loop_count(tag), q.n):
                    one(e)

            units("moe")
            act.wait_ge(S("route_stored"), 16)
            act.wait_ge(S("x_ready"), 2)
            go(SQ[:, :, :], X, ACT.Square).then_inc(S("squared"), 1)
            root("third", RR[:, 0:T])

            def alpha_x(k):
                act.wait_ge(S("h_ready"), 2 + k)
                go(AXS, X, ACT.Copy, scale=ALPHA).then_inc(S("alpha_x"), 1)

            def layer_norm(k, tag):
                for half in range(2):
                    act.wait_ge(S("centered"), 2 * k - 1 + half)
                    ks = slice(4 * half, 4 * half + 4)
                    go(SQ[:, ks, :], AXS[:, ks], ACT.Square).then_inc(S("squared_half"), 1)
                root(tag, RR[:, 0:T])

            alpha_x(1)
            units("ffn0")
            layer_norm(1, "ln0")
            alpha_x(2)

            def indexer():
                b = full("hy_ik")
                freed(go(IK, b[:, 0:T], ACT.Copy), "hy_ik")
                for n in range(8):
                    b = full(f"ix{n}")
                    if n >= 2:
                        act.wait_ge(S("relu_used"), n - 1)
                    freed(go(REL[:, n % 2].rearrange("p a t -> p (a t)"), b, ACT.Relu, scale=0.125), f"ix{n}")

            for n, (kind, c0) in enumerate(hyb_slots):
                if n == 6:
                    indexer()
                b = full(f"hy{n}").rearrange("p (a t) -> p a t", a=2)
                a = 2 * (n % 2)
                if kind == "bq":
                    a = 2 * (n - 8)
                    if n == 8:
                        act.wait_ge(S("pads_zero"), 1)
                    freed(go(CIN[:, a:a + 2, 3:259], b, ACT.Copy), f"hy{n}")
                elif kind == "bz":
                    freed(go(BZ[:, a:a + 2, :], b, ACT.Silu), f"hy{n}")
                elif kind == "av":
                    freed(go(AV[:, :, (n % 2) * HALF:(n % 2 + 1) * HALF], b, ACT.Copy), f"hy{n}")
                else:
                    freed(go({"aq": AQ, "ak": AK, "iq": IQ}[kind][:, a:a + 2, :], b, ACT.Copy), f"hy{n}")
            for n in range(6):
                act.wait_ge(S("conv_done"), n + 1)
                go(QKV[:, 2 * n:2 * n + 2, :], QKV[:, 2 * n:2 * n + 2, :], ACT.Silu).then_inc(S("qkv_silu"), 1)
            def attention(tag, heads, logits, probs, att):
                def exps(h):
                    act.wait_ge(S("att_max"), att_k0[tag] + h + 1)
                    if h >= 2:
                        wait(act, uses[f"{tag}_t{h - 2}"].full)
                    for qt in range(TT):
                        k = 2 * (h % 2) + qt
                        ins = go(probs[:, h % 2, qt, :], logits[:, h % 2, qt, :], ACT.Exp, bias=s_max2[:, k:k + 1],
                                 accum_out=s_sum2[:, k:k + 1])
                    ins.then_inc(S("att_exp"), 1)

                def pair_out(n):
                    b = full(f"{tag}_o{n}")
                    go(MIX[0:64, n, :], b[0:64, 0:T], ACT.Copy)
                    freed(go(MIX[64:128, n, :], b[64:128, T:2 * T], ACT.Copy), f"{tag}_o{n}")

                exps(0)
                for h in range(heads):
                    if h < heads - 1:
                        exps(h + 1)
                    b = full(f"{tag}_t{h}")
                    if h >= 2:
                        if h % 2 == 0:
                            act.wait_ge(S("att_even"), even_k0[tag] + (h - 2) // 2 + 1)
                        else:
                            wait(act, uses[f"{tag}_o{(h - 2) // 2}"].full)
                    freed(go(att[:, h % 2].rearrange("p k t -> p (k t)"), b, ACT.Copy), f"{tag}_t{h}")
                    if h % 2 == 0 and h:
                        pair_out(h // 2 - 1)
                pair_out(heads // 2 - 1)

            attention("dsa", 8, LOG, PRB, ATT_T)

            own("qkv_silu", 6)
            go(L2SQ, QKV[:, 0:8, :], ACT.Square).then_inc(S("qk_squared"), 1)
            act.wait_ge(S("softplus_abs"), 2)
            go(s_tmp[:, 8:16], s_tmp[:, 0:8], ACT.Exp, scale=-1.0).then_inc(S("softplus_exp"), 1)
            go(s_nega, b_alog, ACT.Exp).then_inc(S("a_exp"), 1)
            act.wait_ge(S("iwab_ready"), 1)
            go(s_beta.rearrange("p (t h) -> p t h", t=2), IWAB[:, :, 12:16], ACT.Sigmoid).then_inc(S("beta"), 1)
            root("l2", L2R)
            b = full("gd_rows")
            go(GRW, b[0:4, 0:T], ACT.Copy)
            freed(go(GRB, b[0:4, T:2 * T], ACT.Copy), "gd_rows")
            for n in range(2):
                b = full(f"gd_g{n}")
                go(EGR[:, 4 * n:4 * n + 4, :].rearrange("p a t -> p (a t)"), b, ACT.Exp).then_inc(S("egr"), 1)
            act.wait_ge(S("dec_arg"), 1)
            go(DEC, DEC, ACT.Exp).then_inc(S("dec_exp"), 1)
            act.wait_ge(S("kd_arg"), 1)
            go(s_kd, s_kd, ACT.Exp).then_inc(S("kd_exp"), 1)
            for l in range(7):
                for n in range(2):
                    if l:
                        wait(act, uses[f"gu{l - 1}_{n}"].full)
                    b = full(f"gx{l}_{n}")
                    freed(go(GX[:, 4 * n:4 * n + 4, :].rearrange("p a t -> p (a t)"), b, ACT.Copy), f"gx{l}_{n}")
            b = full("gs_vn0")
            freed(go(VN, b, ACT.Copy), "gs_vn0")
            b = full("gs_s")
            freed(go(ST, b, ACT.Copy), "gs_s")
            b = full("gs_vn1")
            freed(go(VN, b, ACT.Copy), "gs_vn1")
            act.wait_ge(S("delta_out"), 1)
            go(OSQ, OT, ACT.Square).then_inc(S("delta_squared"), 1)
            root("delta", MRI2)
            layer_norm(2, "ln1")
            alpha_x(3)
            units("ffn1")
            layer_norm(3, "ln2")
            alpha_x(4)
            units("ffn2")
            layer_norm(4, "ln3")
            alpha_x(5)

            b = full("ml0")
            freed(go(CQ[:, 0:2, :], b.rearrange("p (a t) -> p a t", a=2), ACT.Copy), "ml0")
            b = full("ml1")
            go(CQ[:, 2, :], b[:, 0:T], ACT.Copy)
            freed(go(CKV[:, 0, :], b[:, T:2 * T], ACT.Copy), "ml1")
            b = full("ml2")
            go(KRAW[0:C_QK, :], b[0:C_QK, T:2 * T], ACT.Copy)
            freed(go(CKV[:, 1, :], b[:, 0:T], ACT.Copy), "ml2")
            own("latent_copied", 3)
            go(CSQ[:, 0:3, :], CQ, ACT.Square)
            go(CSQ[:, 3:5, :], CKV, ACT.Square).then_inc(S("latent_squared"), 1)
            root("latent", MTMP)
            act.wait_ge(S("angles"), 1)
            go(MSIN[0:C_QK], MSIN[0:C_QK], ACT.Sin)
            go(MCOS[0:C_QK], MCOS[0:C_QK], ACT.Sin).then_inc(S("trig"), 1)
            for n in range(8):
                b = full(f"mq{n}")
                if n >= 2:
                    act.wait_ge(S("q_rotated"), n - 1)
                freed(go(MRAW[0:C_QK, n % 2, :], b[0:C_QK, :], ACT.Copy), f"mq{n}")
            for n in range(2):
                for m in range(4):
                    b = full(f"mk{4 * n + m}")
                    h = 8 * n + 2 * m
                    freed(go(KTT[0:DH, h:h + 2, :], b[0:DH, :].rearrange("p (a t) -> p a t", a=2), ACT.Copy),
                          f"mk{4 * n + m}")
                for tt in range(TT):
                    b = full(f"mv{2 * n + tt}")
                    freed(go(VV[:, tt, n * 512:(n + 1) * 512], b, ACT.Copy), f"mv{2 * n + tt}")
            attention("mla", 16, MLOG, MPRB, MATT)
            layer_norm(5, "ln4")
            alpha_x(6)
            units("ffn3")
            layer_norm(6, "ln5")
            for n in range(4):
                b = full(f"fin{n}")
                tt, half = n // 2, n % 2
                freed(go(ar(0, 2, D)[:, tt, half * 512:(half + 1) * 512], b, ACT.Copy), f"fin{n}")

        @block.gpsimd
        def _(pool):
            def spread(dst, src, name):
                pool.dma_start(dst, src.to_broadcast([P] + list(src.shape[1:]))).then_inc(S(name), 16)

            spread(b_dec[:, 0:4], A["ret_decay_fwd"][0:1, :], "spread_in")
            spread(b_dec[:, 4:8], A["ret_decay_bwd"][0:1, :], "spread_in")
            spread(b_rbias, A["router_bias"][0:1, :], "spread_in")
            spread(b_alog, A["gdn_a_log_2"][0:1, :], "spread_in")
            spread(b_dt, A["gdn_dt_bias_2"][0:1, :], "spread_in")
            for k, nm in enumerate(["lambda_q1", "lambda_k1", "lambda_q2", "lambda_k2"]):
                spread(BC[:, 64 * k:64 * k + 64], A[nm][0:1, :], "spread_in")
            spread(POSI[:, :], A["positions_2"][0:1, :], "spread_in")
            pool.dma_start(POSC[:, :], A["positions_2"][0, :].rearrange("(t p) -> p t", p=P),
                           allow_slow_non_contiguous=True).then_inc(S("spread_in"), 16)
            for a in range(ADA_LATE):
                s = a % 2
                if a >= 2:
                    pool.wait_ge(S(f"mod_used{s}"), a // 2)
                pool.dma_start(MR[:, s, :].rearrange("p (k n) -> p k n", k=KT),
                               ada_v[:, :, 2048 + a * HALF:2048 + (a + 1) * HALF]).then_inc(S(f"mod_in{s}"), 16)
                if a == 0:
                    pool.wait_ge(S("h_ready"), 1)
                    pool.dma_start(DIRS[:, :, :, :].rearrange("p a b t -> p (a b t)"), A["k_dirs"][:, :]).then_inc(
                        S("dirs_in"), 16)
            with pool.Fori(0, MOD_SLOTS) as j:
                for l in range(2):
                    pool.wait_ge(S(f"mod_used{l}"), j + ADA_LATE // 2)
                    src = rows(A["mod_w_2"][l])[:, :, bass.ds(j * HALF, HALF)]
                    pool.dma_start(MR[:, l, :].rearrange("p (k n) -> p k n", k=KT), src).then_inc(S(f"mod_in{l}"), 16)
            pool.wait_ge(S("mod_sums"), 1)
            nc.gpsimd.memset(CIN[:, :, 0:3], 0.0).then_inc(S("pads_zero"), 1)
            hw = rows(A["hyb_w_in_2"][0])
            pool.dma_start(IKW[:, :, 0:64], hw[:, :, 2048:2112]).then_inc(S("ikw_in"), 16)
            pool.dma_start(IKW[:, :, 64:136], hw[:, :, 2048:2120]).then_inc(S("ikw_in"), 16)
            pool.dma_start(IKW[:, :, 136:144], hw[:, :, 3656:3664]).then_inc(S("ikw_in"), 16)
            pool.dma_start(KCH, A["k_chunk"].rearrange("p (a n) -> p a n", a=9)).then_inc(S("chunk_in"), 16)
            pool.dma_start(HSEL[0:4], A["k_heads"].rearrange("p (a n) -> p a n", a=4)).then_inc(S("heads_in"), 16)
            pool.wait_ge(S("h_ready"), 5)
            pool.dma_start(KROT, A["k_rot"][:, :]).then_inc(S("rot_in"), 16)

        @block.vector
        def _(dve):
            V = nc.vector
            chain = [0]

            def link(ins):
                chain[0] += 1
                ins.then_inc(S("vector_chain"), 1)
                dve.wait_ge(S("vector_chain"), chain[0])

            def tell(ins, name, n):
                ins.then_inc(S(name), 1)
                dve.wait_ge(S(name), n)

            def full(name):
                wait(dve, uses[name].full)
                return PS[:, uses[name].bank]

            def freed(ins, name):
                tell(ins, *uses[name].free)

            def over(ap, n, at=1):
                return ap.unsqueeze(at).to_broadcast([ap.shape[0], n] + list(ap.shape[1:]))

            def tt_(out_, a, b, op):
                return V.tensor_tensor(out_, a, b, op)

            def ts_(out_, a, s1, op0, s2=None, op1=None):
                if op1 is None:
                    return V.tensor_scalar(out_, a, s1, None, op0)
                return V.tensor_scalar(out_, a, s1, s2, op0, op1)

            def stt(out_, a, s1, b, op0, op1):
                return V.scalar_tensor_tensor(out=out_, in0=a, scalar=s1, in1=b, op0=op0, op1=op1)

            M, AD, SU = ALU.mult, ALU.add, ALU.subtract

            def inverse(ap, name):
                V.reciprocal(ap, ap).then_inc(S("recip"), 1)
                dve.wait_ge(S("rinv"), ROOT[name])

            for n in (0, 2, 4, 6):
                b = full(f"xt{n}")
                tt, half = n // 2, n % 2
                dst = XS[:, tt // 2, 4 * half:4 * half + 4, (tt % 2) * P:(tt % 2 + 1) * P]
                freed(V.tensor_copy(dst, b.rearrange("p (k n) -> p k n", k=4)), f"xt{n}")
            b = full("params")
            V.tensor_copy(COLS[:, :], b[:, 0:392]).then_inc(S("cols_ready"), 1)
            dve.wait_ge(S("cols_ready"), 1)
            dve.wait_ge(S("spread_in"), 16 * 11)
            t = lambda k: s_tmp[:, 8 * k:8 * k + 8]

            def abs_of(x):
                link(ts_(t(1), x, -1.0, M))
                tell(tt_(t(0), x, t(1), ALU.max), "softplus_abs", abs_no[0] + 1)
                abs_no[0] += 1

            abs_no = [0]

            def log1p_exp(k):
                dve.wait_ge(S("softplus_exp"), k)
                link(ts_(t(2), t(1), 2.0, AD))
                link(V.reciprocal(t(2), t(2)))
                link(tt_(t(3), t(1), t(2), M))
                link(tt_(t(4), t(3), t(3), M))
                link(ts_(t(5), t(4), 1.0 / 17, M))
                for c in (15, 13, 11, 9, 7, 5, 3):
                    link(stt(t(5), t(5), 1.0 / c, t(4), AD, M))
                link(stt(t(6), t(5), 1.0, t(3), AD, M))

            abs_of(b_dec)
            for k in range(2):
                q = BC[:, 128 * k:128 * k + 64]
                link(tt_(q, q, BC[:, 128 * k + 64:128 * k + 128], M))
                ins = V.reduce_sum(s_e[:, k:k + 1], q, AX)
                if k == 0:
                    link(ins)
            tell(ins, "lam_sums", 1)
            b = full("ms_first")
            freed(ts_(RR[:, :], b, 1.0 / D, M, NORM_EPS, AD), "ms_first")
            inverse(RR[:, :], "first")
            for s in range(2):
                dst = SQ1[:, :, s * T:(s + 1) * T]
                dve.wait_ge(S("xt_by_scalar"), 4)
                link(tt_(dst, XS[:, s], over(RR[:, s * T:(s + 1) * T], KT), M))
            b = full("ada_col")
            bias = col("ada_b", 0, 16).unsqueeze(2).to_broadcast([P, 16, 2])
            freed(tt_(MODE[:, :, :], b[:, 0:32].rearrange("p (q j) -> p q j", j=2), bias, AD), "ada_col")
            g = col("norm1_g", 0, 8).unsqueeze(2).to_broadcast([P, 8, 2])
            link(stt(MODE[:, 8:16, :], MODE[:, 8:16, :], 1.0, g, AD, M))
            for s in range(2):
                for kt in range(KT):
                    ins = ts_(H[:, kt, s * T:(s + 1) * T], SQ1[:, kt, s * T:(s + 1) * T], MODE[:, 8 + kt, 1 - s:2 - s], M,
                              MODE[:, kt, 1 - s:2 - s], AD)
            tell(ins, "h_ready", 1)
            log1p_exp(1)
            link(ts_(t(0), b_dec, 0.0, ALU.min))
            tell(stt(s_logg, t(6), -2.0, t(0), M, AD), "logg", 1)
            dve.wait_ge(S("lam_exp"), 1)
            link(tt_(s_lam, s_e[:, 1:2], s_e[:, 0:1], SU))
            lam_init = 0.8 - 0.6 * math.exp(0.0)
            link(ts_(s_lam, s_lam, -lam_init, AD))

            def late(a):
                s = a % 2
                dve.wait_ge(S(f"mod_in{s}"), 16 * (a // 2 + 1))
                dve.wait_ge(S("silu_c"), 1)
                if a >= 4:
                    dve.wait_ge(S("ada_acc_used"), a - 3)
                w = MR[:, s, :].rearrange("p (k n) -> p k n", k=KT)
                acc = AACC[:, a % 4, :]
                link(ts_(acc, w[:, 0, :], CS[:, 0, 0:1], M))
                for kt in range(1, KT - 1):
                    link(stt(acc, w[:, kt, :], CS[:, 0, kt:kt + 1], acc, M, AD))
                tell(stt(acc, w[:, KT - 1, :], CS[:, 0, KT - 1:KT], acc, M, AD), f"mod_used{s}", a // 2 + 1)
                V.tensor_copy(acc[:, 0:1], acc[:, 0:1]).then_inc(S("ada_acc"), 1)

            def rope(j):
                dve.wait_ge(S("raw_ready"), j + 1)
                if j < 4:
                    dst = DQ[:, j, :]
                elif j < 8:
                    dst = DK[:, j - 4, T:2 * T]
                elif j < 10:
                    dst = RQ[:, j - 8, :]
                else:
                    dst = RK[:, j - 10, T:2 * T]
                link(tt_(dst, RAW[:, j % 2], COS, M))
                b = full(f"sw{j}")
                freed(tt_(RTMP, b[:, 0:T], SIN, M), f"sw{j}")
                tell(tt_(dst, dst, RTMP, AD), "roped", j + 1)

            for j in range(12):
                rope(j)
                if j in (1, 3, 5, 7):
                    late((j - 1) // 2)
            for a in range(4, ADA_LATE):
                late(a)
            b = full("ada_late")
            freed(tt_(MODA[:, :], b[:, 0:32], col("ada_b", 16, 32), AD), "ada_late")

            def diff_max(u):
                full(f"ds{u}b")
                b0 = uses[f"ds{u}a"].bank
                full(f"ds{u}a")
                k = 2 * (u % 2)
                link(V.reduce_max(s_max[:, k:k + 2], PS[:, b0:b0 + 2, :], AX))
                tell(ts_(s_max[:, k:k + 2], s_max[:, k:k + 2], -0.125, M), "diff_max", u + 1)

            def diff_out(h):
                b = full(f"do{h}")
                freed(V.tensor_copy(MIXED[:, h, :], b[:, 0:T]), f"do{h}")

            diff_max(0)
            for u in range(8):
                if u < 7:
                    diff_max(u + 1)
                dve.wait_ge(S("diff_exp"), u + 1)
                k = 2 * (u % 2)
                link(V.reciprocal(s_r[:, k:k + 2], s_sum[:, k:k + 2]))
                link(tt_(s_r[:, k + 1:k + 2], s_r[:, k + 1:k + 2], s_lam, M))
                link(ts_(PR[:, u % 2, 1, :], PR[:, u % 2, 1, :], s_r[:, k + 1:k + 2], M))
                tell(stt(PR[:, u % 2, 0, :], PR[:, u % 2, 0, :], s_r[:, k:k + 1], PR[:, u % 2, 1, :], M, AD),
                     "diff_weights", u + 1)
                if u >= 2 and u % 2 == 0:
                    diff_out(u // 2 - 1)
            diff_out(3)
            dve.wait_ge(S("dirs_in"), 16)
            for h in range(4):
                dve.wait_ge(S("decay_exp"), h + 1)
                link(tt_(EF[:, 2:4, :], EF[:, 2:4, :], DIRS[:, 0], M))
                link(tt_(EB[:, 2:4, :], EB[:, 2:4, :], DIRS[:, 1], M))
                link(tt_(EF, EF, EB, AD))
                full(f"rs{h}a")
                full(f"rs{h}b")
                b0 = uses[f"rs{h}a"].bank
                if h >= 2:
                    wait(dve, uses[f"ro{h - 2}"].full)
                tell(stt(SD[:, h % 2].rearrange("p k t -> p (k t)"), PS[:, b0:b0 + 2, :].rearrange("p a n -> p (a n)"),
                         0.125, EF.rearrange("p k t -> p (k t)"), M, M), "ret_weights", h + 1)
                if h:
                    b = full(f"ro{h - 1}")
                    freed(V.tensor_copy(MIXED[:, 3 + h, :], b[:, 0:T]), f"ro{h - 1}")
            b = full("ro3")
            freed(V.tensor_copy(MIXED[:, 7, :], b[:, 0:T]), "ro3")
            V.tensor_copy(MIXED[:, 7, 0:1], MIXED[:, 7, 0:1]).then_inc(S("mixed"), 1)
            dve.wait_ge(S("mixed"), 1)
            for n in range(4):
                b = full(f"mn{n}")
                freed(ts_(MRI[:, 2 * n:2 * n + 2, :].rearrange("p a t -> p (a t)"), b, 1.0 / P, M, NORM_EPS, AD), f"mn{n}")
            inverse(MRI, "heads")
            link(tt_(MSQ, MIXED, MRI, M))
            link(ts_(MIX[:, 0:4, :], MSQ[:, 0:4, :], col("dattn_g"), M, 1.0 - lam_init, M))
            wait(dve, uses["rg1"].free)
            tell(stt(MIX[:, 4:8, :], MSQ[:, 4:8, :], col("ret_g"), RG, M, M), "mix_ready", 1)

            def add_products(tag, gate, base, dst):
                for kt in range(KT):
                    if kt % 2 == 0:
                        full(f"{tag}{kt // 2}")
                    ins = stt(dst[:, kt, :], y_of(kt), gate[:, kt:kt + 1], base[:, kt, :], M, AD)
                    if kt % 2:
                        freed(ins, f"{tag}{kt // 2}")

            add_products("wout", MODA[:, 0:8], X, X)

            def rms(name, eps):
                b = full(name)
                freed(ts_(RR[:, 0:T], b[:, 0:T], 1.0 / D, M, eps, AD), name)

            rms("ms_second", NORM_EPS)
            inverse(RR[:, 0:T], "second")
            link(tt_(SQ[:, :, :], X, over(RR[:, 0:T], KT), M))
            link(stt(sc2, MODA[:, 16:24], 1.0, col("norm2_g", 0, 8), AD, M))
            for kt in range(KT):
                ins = ts_(U_IN[:, kt, :], SQ[:, kt, :], sc2[:, kt:kt + 1], M, MODA[:, 8 + kt:9 + kt], AD)
            tell(ins, "h_ready", 2)
            dve.wait_ge(S("router_sigmoid"), 1)
            link(tt_(ROUTE_SEL, ROUTE_S, over(b_rbias, 2), AD))
            G8 = AXS[:, 5, 0:128].rearrange("p (t g k) -> p t g k", t=2, g=8)
            GS = AXS[:, 6, 0:24].rearrange("p (t k) -> p t k", t=2)
            M8 = AXS[:, 6, 32:48].rearrange("p (t k) -> p t k", t=2)
            GM, GN = (AXS[:, 6, 64 + 16 * a:80 + 16 * a].rearrange("p (t k) -> p t k", t=2) for a in range(2))
            for tt in range(TT):
                for gr in range(8):
                    ins = V.max(G8[:, tt, gr, :], ROUTE_SEL[:, tt, 8 * gr:8 * gr + 8])
            link(ins)
            link(V.memset(GS, 3e38))
            link(tt_(GS[:, :, 0:8], G8[:, :, :, 0], G8[:, :, :, 1], AD))
            for tt in range(TT):
                link(V.max(M8[:, tt, :], GS[:, tt, :]))
                link(V.match_replace(out=GS[:, tt, :], in_to_replace=M8[:, tt, :], in_values=GS[:, tt, :],
                                     imm_value=TAKEN))
            link(ts_(GM, GS[:, :, 0:8], -2e38, ALU.is_le))
            link(ts_(GN, GM, -NEG, M, NEG, AD))
            grp = lambda x: x.rearrange("p t (g k) -> p t g k", g=8)
            for tt in range(TT):
                link(tt_(grp(ROUTE_X)[:, tt], grp(ROUTE_SEL)[:, tt], GM[:, tt].unsqueeze(2).to_broadcast([P, 8, 8]), M))
                link(tt_(grp(ROUTE_X)[:, tt], grp(ROUTE_X)[:, tt], GN[:, tt].unsqueeze(2).to_broadcast([P, 8, 8]), AD))
                link(V.max(M8[:, tt, :], ROUTE_X[:, tt, :]))
                link(V.match_replace(out=ROUTE_X[:, tt, :], in_to_replace=M8[:, tt, :], in_values=ROUTE_X[:, tt, :],
                                     imm_value=TAKEN))
            link(ts_(ROUTE_X, ROUTE_X, -2e38, ALU.is_le))
            link(tt_(ROUTE_W, ROUTE_X, ROUTE_S, M))
            link(V.reduce_sum(s_r2[:, 0:2], ROUTE_W, AX))
            link(V.reciprocal(s_r2[:, 0:2], s_r2[:, 0:2]))
            for tt in range(TT):
                ins = ts_(ROUTE_W[:, tt, :], ROUTE_W[:, tt, :], s_r2[:, tt:tt + 1], M, 2.5, M)
            tell(ins, "route_weights", 1)

            def mod_item(l, j, i=None):
                n = 0 if i is None else i
                dve.wait_ge(S(f"mod_in{l}"), 16 * (ADA_LATE // 2 + j + 1 + n))
                w = MR[:, l, :].rearrange("p (k n) -> p k n", k=KT)
                acc = MACC[:, l, j, :] if i is None else MACC[:, l, bass.ds(j + i, 1), :].rearrange("p o n -> p (o n)")
                k0 = (KT - 1) * (2 * j + l)
                V.tensor_scalar(acc, w[:, 0, :], CS[:, 2, 0:1], None, M).then_inc(S("mod_chain"), 1)
                for kt in range(1, KT):
                    dve.wait_ge(S("mod_chain"), k0 + kt + 2 * (KT - 1) * n)
                    ins = stt(acc, w[:, kt, :], CS[:, 2, kt:kt + 1], acc, M, AD)
                    ins.then_inc(S("mod_chain") if kt < KT - 1 else S(f"mod_used{l}"), 1)

            def units(tag):
                q = ph[tag]
                moe = tag == "moe"

                def one(e, i=None):
                    n = 0 if i is None else i
                    u = uses[f"{tag}_up{e}"]
                    dve.wait_ge(S("silu_gate"), q.unit0 + e + 1 + 2 * n)
                    dve.wait_ge(S(u.full[0]), u.full[1] + n)
                    if q.unit0 + e >= 2:
                        dve.wait_ge(S("units_down"), q.unit0 + e - 1 + 2 * n)
                    s, h = SIL[:, e % 2], HID[:, e % 2]
                    flat = lambda x: x.rearrange("p a t -> p (a t)")
                    if moe and e < N_EXP:
                        tt_(flat(s), flat(s), PS[:, u.bank], M).then_inc(S("gated"), 1)
                        dve.wait_ge(S("gated"), e + 1 + 2 * n)
                        dve.wait_ge(S(f"route_in{e % 2}"), 16 * (e // 2 + 1 + n))
                        tt_(h, s, over(GW[:, e % 2, :], 2), M).then_inc(S("hidden_ready"), 1)
                    else:
                        tt_(flat(h), flat(s), PS[:, u.bank], M).then_inc(S("hidden_ready"), 1)

                for e in range(PEELED):
                    one(e)
                    if moe:
                        mod_item(0, e)
                        mod_item(1, e)
                with dve.Fori(0, loop_count(tag)) as i:
                    one(PEELED, i)
                    if moe:
                        mod_item(0, PEELED, i)
                    one(PEELED + 1, i)
                    if moe:
                        mod_item(1, PEELED, i)
                for e in range(PEELED + 2 * loop_count(tag), q.n):
                    one(e)
                    if moe:
                        mod_item(0, e - 30)
                        mod_item(1, e - 30)
                if moe:
                    for j in range(q.n - 30, MOD_SLOTS):
                        mod_item(0, j)
                        mod_item(1, j)
                    for l in range(2):
                        dve.wait_ge(S(f"mod_used{l}"), ADA_LATE // 2 + MOD_SLOTS)
                    V.memset(small(250), 0.0).then_inc(S("mod_acc"), 2 * MOD_SLOTS)

            wait(dve, uses["routeT"].free)
            units("moe")
            add_products("moe_y", MODA[:, 24:32], X, X)
            b = full("mod_first")
            freed(tt_(MODC[:, 0, 0:24], b[:, 0:24], col("mod_b0", 0, 24), AD), "mod_first")
            rms("ms_third", NORM_EPS)
            inverse(RR[:, 0:T], "third")
            link(tt_(X, X, over(RR[:, 0:T], KT), M))
            for kt in range(KT):
                ins = ts_(X[:, kt, :], X[:, kt, :], col("final_g", kt), M)
            link(ins)

            def modulate(k):
                l, sub = k // 3, k % 3
                m = lambda which: MODC[:, l, 24 * sub + 8 * which:24 * sub + 8 * which + 8]
                c = 1.0 if sub == 1 else 0.5
                link(ts_(g1c, m(2), 1.0, AD, c, M))
                link(ts_(u_sc, m(1), 1.0, AD))
                for kt in range(KT):
                    ins = ts_(U_IN[:, kt, :], X[:, kt, :], u_sc[:, kt:kt + 1], M, m(0)[:, kt:kt + 1], AD)
                tell(ins, "h_ready", 3 + k)

            modulate(0)

            def add_bias(l, lo):
                b = full(f"mod_sum{l}")
                freed(tt_(MODC[:, l, lo:72], b[:, lo:72], col(f"mod_b{l}", lo, 72 - lo), AD), f"mod_sum{l}")

            add_bias(0, 24)

            def layer_norm(k, tag, ytag):
                dve.wait_ge(S("alpha_x"), k)
                add_products(ytag, g1c, AXS, AXS)
                b = full(f"{tag}_mean")
                freed(ts_(MEAN[:, :], b[:, 0:T], 1.0 / D, M), f"{tag}_mean")
                for half in range(2):
                    ks = slice(4 * half, 4 * half + 4)
                    tell(tt_(AXS[:, ks], AXS[:, ks], over(MEAN[:, :], 4), SU), "centered", 2 * k - 1 + half)
                rms(f"{tag}_ms", LN_EPS)
                inverse(RR[:, 0:T], tag)
                link(tt_(AXS, AXS, over(RR[:, 0:T], KT), M))
                for kt in range(KT):
                    i_ = 8 * (k - 1) + kt
                    ins = ts_(X[:, kt, :], AXS[:, kt, :], col("ln_g", i_), M, col("ln_b", i_), AD)
                if k < 6:
                    link(ins)
                    modulate(k)
                else:
                    tell(ins, "result_features", 1)

            units("ffn0")
            layer_norm(1, "ln0", "ffn0_y")
            add_bias(1, 0)
            V.memset(small(251), 0.0).then_inc(S("mod_sums"), 1)

            link(ts_(CHKF[:, :].bitcast(I32), POSI[:, :], 6, ALU.arith_shift_right))
            link(V.tensor_copy(CHKF[:, :], CHKF[:, :].bitcast(I32)))
            link(V.tensor_copy(POSF, POSI[:, :]))
            link(ts_(s_chc.bitcast(I32), POSC[:, :], 6, ALU.arith_shift_right))
            link(V.tensor_copy(s_chc, s_chc.bitcast(I32)))
            link(V.tensor_copy(s_posc, POSC[:, :]))

            def visible(dst):
                for qt in range(TT):
                    ins = ts_(dst[:, qt, :], CHKF[:, :], s_chc[:, qt:qt + 1], ALU.is_le)
                link(ins)

            b = full("hy_iw")
            freed(V.tensor_copy(IWAB, b[:, 0:32].rearrange("p (t n) -> p t n", t=2)), "hy_iw")
            link(ts_(IWAB[:, :, 0:8], IWAB[:, :, 0:8], float(np.float32(IDX_HEADS ** -0.5)), M))
            for n in range(8):
                dve.wait_ge(S("relu_done"), n + 1)
                for qt in range(TT):
                    r = REL[:, n % 2, qt, :]
                    if n == 0:
                        ins = ts_(SCORE[:, qt, :], r, IWAB[:, qt, 0:1], M)
                    else:
                        ins = stt(SCORE[:, qt, :], r, IWAB[:, qt, n:n + 1], SCORE[:, qt, :], M, AD)
                tell(ins, "relu_used", n + 1)
            VIS = DISTP
            visible(VIS)
            link(ts_(NM, VIS, -NEG, M, NEG, AD))
            link(tt_(SCORE, SCORE, VIS, M))
            link(tt_(SCORE, SCORE, NM, AD))
            for qt in range(TT):
                src = SCORE[:, qt, :]
                for r in range(TOPK // 8):
                    link(V.max(MAX8, src))
                    link(V.match_replace(out=WORK, in_to_replace=MAX8, in_values=src, imm_value=TAKEN))
                    src = WORK
                link(stt(NM[:, qt, :], WORK, -2e38, VIS[:, qt, :], ALU.is_le, M))
            link(ts_(NM, NM, -NEG, M, NEG, AD))
            for qt in range(TT):
                link(ts_(DISTP[:, qt, :], POSF, s_posc[:, qt:qt + 1], SU))
                link(ts_(WORK, DISTP[:, qt, :], -1.0, M))
                link(tt_(DISTP[:, qt, :], DISTP[:, qt, :], WORK, ALU.max))

            for c in range(12):
                if c % 2 == 0:
                    dve.wait_ge(S("cin_ready"), c // 2 + 1)
                if c == 0:
                    dve.wait_ge(S("pads_zero"), 1)
                link(ts_(QKV[:, c, :], CIN[:, c, 0:T], col("conv", c), M))
                for k in range(1, 4):
                    ins = stt(QKV[:, c, :], CIN[:, c, k:k + T], col("conv", 12 * k + c), QKV[:, c, :], M, AD)
                    if k < 3 or c % 2 == 0:
                        link(ins)
                if c % 2:
                    tell(ins, "conv_done", c // 2 + 1)

            def attention(tag, heads, logits, probs, scale, bias):
                k0 = att_k0[tag]

                def soft(h):
                    bb = bias(h)
                    b = full(f"{tag}_s{h}")
                    lg = logits[:, h % 2].rearrange("p a t -> p (a t)")
                    freed(stt(lg, b, scale, bb.rearrange("p a t -> p (a t)"), M, AD), f"{tag}_s{h}")
                    k = 2 * (h % 2)
                    link(V.reduce_max(s_max2[:, k:k + 2], logits[:, h % 2], AX))
                    tell(ts_(s_max2[:, k:k + 2], s_max2[:, k:k + 2], -1.0, M), "att_max", k0 + h + 1)

                soft(0)
                for h in range(heads):
                    if h < heads - 1:
                        soft(h + 1)
                    dve.wait_ge(S("att_exp"), k0 + h + 1)
                    k = 2 * (h % 2)
                    link(V.reciprocal(s_r2[:, k:k + 2], s_sum2[:, k:k + 2]))
                    p_ = probs[:, h % 2]
                    tell(tt_(p_, p_, s_r2[:, k:k + 2].unsqueeze(2).to_broadcast([P, 2, T]), M), "att_weights", k0 + h + 1)

            def alibi(h):
                link(stt(BIAS[:, h % 2].rearrange("p a t -> p (a t)"), DISTP.rearrange("p a t -> p (a t)"),
                         -float(np.float32(2.0 ** (-(h + 1)))), NM.rearrange("p a t -> p (a t)"), M, AD))
                return BIAS[:, h % 2]

            attention("dsa", 8, LOG, PRB, 0.125, alibi)

            dve.wait_ge(S("iwab_ready"), 1)
            link(tt_(t(6).rearrange("p (t h) -> p t h", t=2), IWAB[:, :, 8:12], over(b_dt, 2), AD))
            link(V.tensor_copy(s_kd, t(6)))
            abs_of(s_kd)
            log1p_exp(2)
            link(ts_(s_kd, s_kd, 0.0, ALU.max))
            link(stt(s_g, t(6), 2.0, s_kd, M, AD))
            dve.wait_ge(S("a_exp"), 1)
            gv = s_g.rearrange("p (t h) -> p t h", t=2)
            dve.wait_ge(S("beta"), 1)
            tell(stt(gv, gv, -1.0, over(s_nega, 2), M, M), "gates", 1)
            for n in range(4):
                b = full(f"l2_{n}")
                freed(ts_(L2R[:, 2 * n:2 * n + 2, :].rearrange("p a t -> p (a t)"), b, 1.0, M, NORM_EPS, AD), f"l2_{n}")
            inverse(L2R, "l2")
            flat = lambda x: x.rearrange("p a t -> p (a t)")
            link(stt(flat(QKV[:, 0:4, :]), flat(QKV[:, 0:4, :]), float(np.float32(P ** -0.5)), flat(L2R[:, 0:4, :]), M, M))
            tell(tt_(flat(QKV[:, 4:8, :]), flat(QKV[:, 4:8, :]), flat(L2R[:, 4:8, :]), M), "qk_normed", 1)
            b = full("gd_cols")
            freed(V.tensor_copy(s_gc, b[:, 0:8]), "gd_cols")
            gc_pr = s_gc.rearrange("p (t h) -> p h t", t=2)
            for n in range(2):
                b = full(f"gd_g{n}")
                dve.wait_ge(S("egr"), n + 1)
                for m in range(4):
                    h, tt = 2 * n + m // 2, m % 2
                    ins = ts_(DEC[:, 4 * n + m, :], b[:, m * P:(m + 1) * P], s_gc[:, 4 * tt + h:4 * tt + h + 1], SU, 0.0,
                              ALU.min)
                if n:
                    tell(ins, "dec_arg", 1)
                lastc = b.rearrange("p (h t n) -> p h t n", h=2, t=2)[:, :, :, P - 1]
                freed(tt_(s_kd[:, 4 * n:4 * n + 4].rearrange("p (h t) -> p h t", h=2), lastc, gc_pr[:, 2 * n:2 * n + 2, :],
                          SU), f"gd_g{n}")
            dve.wait_ge(S("chunk_in"), 16)
            dve.wait_ge(S("dec_exp"), 1)
            link(tt_(DEC, DEC, over(KCH[:, 7, :], 8), M))
            four = lambda x, n: x[:, 4 * n:4 * n + 4, :].rearrange("p a t -> p (a t)")
            link(tt_(QG, QKV[:, 0:4, :].rearrange("p h (t n) -> p (h t) n", t=2), EGR, M))
            for n in range(2):
                b = full(f"gd_kk{n}")
                freed(tt_(four(MT, n), four(DEC, n), b, M), f"gd_kk{n}")
                b = full(f"gd_b{n}")
                link(tt_(four(MT, n), four(MT, n), b, M))
                freed(tt_(four(KBG, n), flat(QKV[:, 4 + 2 * n:6 + 2 * n, :]), b, M), f"gd_b{n}")
                b = full(f"gd_qk{n}")
                freed(tt_(four(GA, n), four(DEC, n), b, M), f"gd_qk{n}")
            link(tt_(MT, MT, over(KCH[:, 8, :], 8), M))
            link(V.tensor_copy(GD, over(IDN, 8)))
            link(V.tensor_copy(GU, over(IDN, 8)))

            def level_mask(l, n):
                h4 = slice(4 * n, 4 * n + 4)
                tell(tt_(GOFF[:, h4], MT[:, h4], over(KCH[:, l, :], 4), M), "inv_masked", 2 * l + n + 1)

            level_mask(0, 0)
            level_mask(0, 1)
            link(tt_(KBG, KBG, EGR, M))
            for n in range(2):
                b = full(f"gd_v{n}")
                for m in range(4):
                    h, tt = 2 * n + m // 2, m % 2
                    ins = ts_(VB[:, 4 * n + m, :], b[:, m * P:(m + 1) * P], s_beta[:, 4 * tt + h:4 * tt + h + 1], M)
                freed(ins, f"gd_v{n}")
            dve.wait_ge(S("kd_exp"), 1)
            b = full("gd_k0")
            for h in range(4):
                ins = ts_(KTOK[:, h, :], b[:, h * P:(h + 1) * P], s_kd[:, 2 * h:2 * h + 1], M)
            freed(ins, "gd_k0")
            V.memset(small(252), 0.0).then_inc(S("gd_operands"), 1)
            for l in range(7):
                for n in range(2):
                    wait(dve, uses[f"gx{l}_{n}"].full)
                    if l < 6:
                        level_mask(l + 1, n)
                for n in range(2):
                    wait(dve, uses[f"gu{l}_{n}"].full)
                    if l < 6:
                        b = full(f"gd{l}_{n}")
                        freed(tt_(four(GD, n), four(GD, n), b, SU), f"gd{l}_{n}")
                    freed(tt_(four(GU, n), four(GU, n), PS[:, uses[f"gu{l}_{n}"].bank], SU), f"gu{l}_{n}")
            b = full("gs_o0")
            tok4 = lambda x: x.rearrange("p (h n) -> p h n", h=4)
            freed(V.tensor_copy(OT[:, :, 0:P], tok4(b)), "gs_o0")
            b = full("gs_r1")
            VBh = VB.rearrange("p (h t) n -> p h t n", t=2)[:, :, 1, :]
            freed(tt_(tok4(RS_), VBh, tok4(b), SU), "gs_r1")
            b = full("gs_o1")
            freed(V.tensor_copy(OT[:, :, P:2 * P], tok4(b)), "gs_o1")
            for n in range(2):
                b = full(f"gn{n}")
                freed(ts_(flat(MRI2[:, 2 * n:2 * n + 2, :]), b, 1.0 / P, M, NORM_EPS, AD), f"gn{n}")
            inverse(MRI2, "delta")
            link(tt_(OT, OT, MRI2, M))
            wait(dve, uses["dsa_o3"].free)
            dve.wait_ge(S("bz_silu"), 2)
            tell(stt(MIX[:, 4:8, :], OT, col("gdn_g"), BZ, M, M), "mix_ready", 2)
            layer_norm(2, "ln1", "hout")
            units("ffn1")
            layer_norm(3, "ln2", "ffn1_y")
            units("ffn2")
            layer_norm(4, "ln3", "ffn2_y")

            dve.wait_ge(S("rot_in"), 16)
            R96 = slice(0, C_QK)
            ANG, NN = MLOG[R96, 0, 0, :], MLOG[R96, 0, 1, :]
            link(ts_(ANG, POSF[R96], KROT[R96, C_QK:C_QK + 1], M))
            magic = 1.5 * 2.0 ** 23
            c1 = 6.28125
            c2 = math.floor((2 * math.pi - c1) * 2 ** 19) / 2 ** 19
            c3 = float(np.float32(2 * math.pi - c1 - c2))
            link(ts_(NN, ANG, float(np.float32(1 / (2 * math.pi))), M, magic, AD))
            link(ts_(NN, NN, -magic, AD))
            for c in (c1, c2, c3):
                link(stt(ANG, NN, -c, ANG, M, AD))
            link(ts_(MSIN[R96], ANG, pi32, ALU.min, -pi32, ALU.max))
            link(ts_(NN, ANG, -1.0, M))
            link(tt_(NN, ANG, NN, ALU.max))
            tell(ts_(MCOS[R96], NN, -1.0, M, float(np.float32(math.pi / 2)), AD), "angles", 1)
            visible(MNM)
            link(ts_(MNM, MNM, -NEG, M, NEG, AD))
            b = full("mq_ms")
            freed(ts_(MTMP[:, 0:T], b[:, 0:T], 1.0 / 384, M, NORM_EPS, AD), "mq_ms")
            b = full("mkv_ms")
            freed(ts_(MTMP[:, T:2 * T], b[:, 0:T], 1.0 / 256, M, NORM_EPS, AD), "mkv_ms")
            inverse(MTMP, "latent")
            for kt in range(3):
                link(stt(CQ[:, kt, :], CQ[:, kt, :], col("q_g", kt), MTMP[:, 0:T], M, M))
            for kt in range(2):
                ins = stt(CKV[:, kt, :], CKV[:, kt, :], col("kv_g", kt), MTMP[:, T:2 * T], M, M)
            tell(ins, "latent_normed", 1)
            dve.wait_ge(S("trig"), 1)
            rr = slice(64, 96)
            b = full("mk_rot")
            link(tt_(KRAW[rr], KRAW[rr], MCOS[rr], M))
            freed(tt_(MTMP[rr, 0:T], b[rr, 0:T], MSIN[rr], M), "mk_rot")
            tell(tt_(KTT[rr], over(KRAW[rr], 16), over(MTMP[rr, 0:T], 16), AD), "k_rotated", 1)
            for n in range(8):
                dve.wait_ge(S("mq_raw"), n + 1)
                dst = QT[R96, 2 * n:2 * n + 2, :]
                two = lambda x: x.rearrange("p (a t) -> p a t", a=2)
                link(tt_(dst, two(MRAW[R96, n % 2, :]), over(MCOS[R96], 2), M))
                b = full(f"mr{n}")
                freed(tt_(two(MTMP[R96]), two(b[R96]), over(MSIN[R96], 2), M), f"mr{n}")
                tell(tt_(dst, dst, two(MTMP[R96]), AD), "q_rotated", n + 1)
            attention("mla", 16, MLOG, MPRB, float(np.float32(C_QK ** -0.5)), lambda h: MNM)
            wait(dve, uses["mla_o7"].free)
            V.memset(small(254), 0.0).then_inc(S("mix_ready"), 1)
            layer_norm(5, "ln4", "mout")
            units("ffn3")
            layer_norm(6, "ln5", "ffn3_y")


INPUTS = ["x", "ctx", "ada_w", "w_in", "lambda_q1", "lambda_k1", "lambda_q2", "lambda_k2", "ret_decay_fwd",
          "ret_decay_bwd", "w_out", "router_w", "router_bias", "exp_w1", "exp_w3", "exp_w2", "shared_w1", "shared_w3",
          "shared_w2", "positions_2", "mod_w_2", "ffn_w_gate_2", "ffn_w_up_2", "ffn_w_down_2", "hyb_w_in_2",
          "hyb_w_out_2", "gdn_a_log_2", "gdn_dt_bias_2", "mla_w_in_2", "mla_w_q_up_2", "mla_w_kv_up_2", "mla_w_out_2"]
ROWS = {"norm1_g": "norm1_g", "norm2_g": "norm2_g", "final_g": "final_norm_g", "c": "c", "c_ctx": "c_ctx", "c2": "c_2",
        "ada_b": "ada_b", "dattn_g": "dattn_norm_g", "ret_g": "ret_norm_g", "gdn_g": "gdn_norm_g_2",
        "q_g": "mla_q_norm_g_2", "kv_g": "mla_kv_norm_g_2", "ln_g": "ln_g_2", "ln_b": "ln_b_2", "conv": "gdn_conv_w_2"}


def kernel(**inputs):
    import concourse.bacc as bacc
    from concourse.bass_utils import run_bass_kernel_spmd

    nc = bacc.Bacc("TRN2", target_bir_lowering=False, num_devices=1)
    arrays, aps = {}, {}

    def give(name, a):
        a = np.ascontiguousarray(a)
        arrays[f"in_{name}"] = a
        aps[name] = nc.dram_tensor(f"in_{name}", a.shape, mybir.dt.from_np(a.dtype), kind="ExternalInput").ap()

    for name in INPUTS:
        give(name, np.asarray(inputs[name]))
    for name, src in ROWS.items():
        give("rows_" + name, np.asarray(inputs[src]).reshape(-1, P))
    for l in range(2):
        give(f"rows_mod_b{l}", np.asarray(inputs["mod_b_2"])[l].reshape(-1, P))
    for name, a in shape_constants().items():
        give(name, a)
    out = nc.dram_tensor("out", (1, T, D), mybir.dt.float32, kind="ExternalOutput").ap()
    route_rows = nc.dram_tensor("route_rows", (N_EXP, T), mybir.dt.float32, kind="Internal").ap()
    build(nc, aps, out, route_rows)
    r = run_bass_kernel_spmd(nc, [arrays], core_ids=[0])
    return r.results[0]["out"]
```
